# Optimizing a Trainium2 kernel written in Bass

```python
import jax, jax.numpy as jnp
from jax import lax
import numpy as np

D_MODEL = 2048
BATCH = 1
SEQ = 256
DEPTH = 1
DEC_BATCH = 8
DEC_SEQ = 1
PAST_LEN = 2048
PAGE_SIZE = 128

POOL_WIDTH = D_MODEL // 2
POOL_WINDOWS = (2, 4, 8, 16)
N_POOL_GROUPS = len(POOL_WINDOWS)
POOL_GROUP = POOL_WIDTH // N_POOL_GROUPS
POOL_HIST = max(POOL_WINDOWS) - 1
CONV_WIDTH = D_MODEL // 2
CONV_K = 3
CONV_HIST = CONV_K - 1
D_FF = 4 * D_MODEL
IN_WIDTH = POOL_WIDTH + 3 * CONV_WIDTH + 2 * D_MODEL
N_ADA = 6
ALPHA = (2 * DEPTH) ** 0.25
BETA = (8 * DEPTH) ** -0.25
LN_EPS = 1e-5

kernel_name = "gated_pool_shortconv_deepnorm_adaln_step"

def _layernorm(x, g, b):
    xf = x.astype(jnp.float32)
    mu = jnp.mean(xf, axis=-1, keepdims=True)
    var = jnp.mean(jnp.square(xf - mu), axis=-1, keepdims=True)
    y = (xf - mu) * lax.rsqrt(var + LN_EPS)
    return (y * g.astype(jnp.float32) + b.astype(jnp.float32)).astype(x.dtype)

def _pool_mixer(z, hist, pos, grp_w, scale):
    L = z.shape[1]
    zz = jnp.concatenate([hist.astype(z.dtype), z], axis=1)
    zf = zz.astype(jnp.float32)
    cs = jnp.concatenate([jnp.zeros_like(zf[:, :1]), jnp.cumsum(zf, axis=1)], axis=1)
    upper = cs[:, POOL_HIST + 1:]
    means = []
    for g, w in enumerate(POOL_WINDOWS):
        sl = slice(g * POOL_GROUP, (g + 1) * POOL_GROUP)
        lower = cs[:, POOL_HIST + 1 - w: POOL_HIST + 1 - w + L, sl]
        cnt = jnp.minimum(w, pos + 1).astype(jnp.float32)
        means.append((upper[..., sl] - lower) / cnt[None, :, None])
    pooled = (jnp.concatenate(means, axis=-1) - z.astype(jnp.float32)).astype(z.dtype)
    B = z.shape[0]
    pg = pooled.reshape(B, L, N_POOL_GROUPS, POOL_GROUP)
    out = jnp.einsum('blgi,gio->blgo', pg, grp_w).reshape(B, L, POOL_WIDTH) * scale
    return out, zz[:, -POOL_HIST:]

def _short_conv(v, hist, conv_w):
    L = v.shape[1]
    vv = jnp.concatenate([hist.astype(v.dtype), v], axis=1)
    out = conv_w[0] * vv[:, 0:L]
    for k in range(1, CONV_K):
        out = out + conv_w[k] * vv[:, k:k + L]
    return out, vv[:, -CONV_HIST:]

def _layer(x, c, pool_hist, conv_hist, pos, w_ada, b_ada, w_in, pool_grp_w, pool_scale, conv_w,
           w_pool_up, w_conv_up, w_o, ln1_g, ln1_b, w_ff1, b_ff1, w_ff2, b_ff2, ln2_g, ln2_b):
    ada = (c @ w_ada + b_ada)[:, None, :]
    sh1, sc1, g1, sh2, sc2, g2 = jnp.split(ada, N_ADA, axis=-1)
    u = x * (1 + sc1) + sh1
    proj = u @ w_in
    o1 = POOL_WIDTH
    o2 = o1 + CONV_WIDTH
    o3 = o2 + CONV_WIDTH
    o4 = o3 + CONV_WIDTH
    o5 = o4 + D_MODEL
    z_p, x_c, b_c, c_c, gate_p, gate_c = jnp.split(proj, [o1, o2, o3, o4, o5], axis=-1)
    y_p, new_pool = _pool_mixer(z_p, pool_hist, pos, pool_grp_w, pool_scale)
    y_p = y_p @ w_pool_up
    y_c, new_conv = _short_conv(c_c * x_c, conv_hist, conv_w)
    y_c = (b_c * y_c) @ w_conv_up
    mixed = (jax.nn.sigmoid(gate_p) * y_p + jax.nn.sigmoid(gate_c) * y_c) @ w_o
    x = _layernorm(ALPHA * x + g1 * mixed, ln1_g, ln1_b)
    u2 = x * (1 + sc2) + sh2
    h = jnp.square(jax.nn.relu(u2 @ w_ff1 + b_ff1))
    x = _layernorm(ALPHA * x + g2 * (h @ w_ff2 + b_ff2), ln2_g, ln2_b)
    return x, new_pool, new_conv

def setup_inputs(seed: int = 0) -> dict:
    key = jax.random.key(seed)
    ks = jax.random.split(key, 32)
    f32 = jnp.float32

    def nrm(k, shape, s):
        return jax.random.normal(k, shape, f32) * s

    d = {}
    d["x_prompt"] = nrm(ks[0], (BATCH, SEQ, D_MODEL), 1.0)
    d["x_sample"] = nrm(ks[1], (DEC_BATCH, DEC_SEQ, D_MODEL), 1.0)
    d["state_pool"] = nrm(ks[2], (DEPTH, DEC_BATCH, POOL_HIST, POOL_WIDTH), 1.0)
    d["state_conv"] = nrm(ks[3], (DEPTH, DEC_BATCH, CONV_HIST, CONV_WIDTH), 1.0)
    d["c_prompt"] = nrm(ks[4], (BATCH, D_MODEL), 1.0)
    d["c_sample"] = nrm(ks[5], (DEC_BATCH, D_MODEL), 1.0)
    d["w_ada"] = nrm(ks[6], (DEPTH, D_MODEL, N_ADA * D_MODEL), 0.3 * D_MODEL ** -0.5)
    d["b_ada"] = nrm(ks[7], (DEPTH, N_ADA * D_MODEL), 0.02)
    d["w_in"] = nrm(ks[8], (DEPTH, D_MODEL, IN_WIDTH), D_MODEL ** -0.5)
    d["pool_grp_w"] = nrm(ks[9], (DEPTH, N_POOL_GROUPS, POOL_GROUP, POOL_GROUP), POOL_GROUP ** -0.5)
    d["pool_scale"] = 1.0 + nrm(ks[10], (DEPTH, POOL_WIDTH), 0.1)
    d["conv_w"] = nrm(ks[11], (DEPTH, CONV_K, CONV_WIDTH), CONV_K ** -0.5)
    d["w_pool_up"] = nrm(ks[12], (DEPTH, POOL_WIDTH, D_MODEL), POOL_WIDTH ** -0.5)
    d["w_conv_up"] = nrm(ks[13], (DEPTH, CONV_WIDTH, D_MODEL), CONV_WIDTH ** -0.5)
    d["w_o"] = nrm(ks[14], (DEPTH, D_MODEL, D_MODEL), BETA * D_MODEL ** -0.5)
    d["ln1_g"] = 1.0 + nrm(ks[15], (DEPTH, D_MODEL), 0.05)
    d["ln1_b"] = nrm(ks[16], (DEPTH, D_MODEL), 0.02)
    d["w_ff1"] = nrm(ks[17], (DEPTH, D_MODEL, D_FF), D_MODEL ** -0.5)
    d["b_ff1"] = nrm(ks[18], (DEPTH, D_FF), 0.02)
    d["w_ff2"] = nrm(ks[19], (DEPTH, D_FF, D_MODEL), BETA * D_FF ** -0.5)
    d["b_ff2"] = nrm(ks[20], (DEPTH, D_MODEL), 0.02)
    d["ln2_g"] = 1.0 + nrm(ks[21], (DEPTH, D_MODEL), 0.05)
    d["ln2_b"] = nrm(ks[22], (DEPTH, D_MODEL), 0.02)
    return d

def reference(x_prompt, x_sample, state_pool, state_conv, c_prompt, c_sample,
              w_ada, b_ada, w_in, pool_grp_w, pool_scale, conv_w, w_pool_up, w_conv_up, w_o,
              ln1_g, ln1_b, w_ff1, b_ff1, w_ff2, b_ff2, ln2_g, ln2_b):
    pos_prompt = jnp.arange(SEQ, dtype=jnp.int32)
    pos_sample = PAST_LEN + jnp.arange(x_sample.shape[1], dtype=jnp.int32)
    nb = x_prompt.shape[0]
    zero_pool = jnp.zeros((nb, POOL_HIST, POOL_WIDTH), x_prompt.dtype)
    zero_conv = jnp.zeros((nb, CONV_HIST, CONV_WIDTH), x_prompt.dtype)
    xp, xs = x_prompt, x_sample
    pool_p, conv_p, pool_s, conv_s = [], [], [], []
    for l in range(DEPTH):
        lw = (w_ada[l], b_ada[l], w_in[l], pool_grp_w[l], pool_scale[l], conv_w[l],
              w_pool_up[l], w_conv_up[l], w_o[l], ln1_g[l], ln1_b[l],
              w_ff1[l], b_ff1[l], w_ff2[l], b_ff2[l], ln2_g[l], ln2_b[l])
        xp, npp, ncp = _layer(xp, c_prompt, zero_pool, zero_conv, pos_prompt, *lw)
        xs, nps, ncs = _layer(xs, c_sample, state_pool[l], state_conv[l], pos_sample, *lw)
        pool_p.append(npp)
        conv_p.append(ncp)
        pool_s.append(nps)
        conv_s.append(ncs)
    return (xp, xs, jnp.stack(pool_p), jnp.stack(conv_p), jnp.stack(pool_s), jnp.stack(conv_s))


_drawn_inputs = setup_inputs


def setup_inputs(seed=0):
    import zlib

    import numpy as np

    out = dict(_drawn_inputs(seed))
    spreads = {}
    factors = {'pool_scale': 7.652, 'ln1_b': 2.88, 'b_ff1': 8.0, 'b_ff2': 8.0, 'ln2_b': 2.831}
    for name, (base, spread) in spreads.items():
        noise = np.random.default_rng([zlib.crc32(name.encode()), seed]).standard_normal(out[name].shape)
        drawn = base * np.exp(spread * noise) if base else spread * noise
        out[name] = __import__('jax').numpy.asarray(drawn.astype(out[name].dtype))
    for name, factor in factors.items():
        out[name] = (out[name] * factor).astype(out[name].dtype)
    return out
```

```python
from contextlib import ExitStack

import concourse.bass as bass
from concourse import mybir

F32 = mybir.dt.float32
F32R = mybir.dt.float32r
ALU = mybir.AluOpType
ACT = mybir.ActivationFunctionType
ds = bass.ds

P = 128
D = 2048
PROMPT = 256
NS = 8
TOK = PROMPT + NS
SEQS = 1 + NS
NT = D // P
PT = NT // 2
POOL_W = (2, 4, 8, 16)
HIST = max(POOL_W) - 1
CH = 2
TAPS = 3
FF = 4 * D
EPS = 1e-5
ALPHA = 2.0 ** 0.25

KC = 4
UC = 512
MT = UC // P
US = KC * UC
RAW = 4
HL = 2
BANKS = 4
AR = 2
ADA_UNITS = D // P // KC
GW = 512

U_GRP = 64
U_UP = U_GRP + 4
U_WO = U_UP + 16
U_FF = U_WO + 16
T_GRP = 4 * U_GRP
T_UP = T_GRP + PT
T_WO = T_UP + 2 * NT
T_FF = T_WO + NT
A_LAST = 14
A_UP = 18
A_WO = 21

V_BFF1, V_PSCALE, V_CONV, V_G1, V_B1 = 0, 64, 72, 96, 112
V_BADA, V_BFF2, V_G2 = 128, 224, 240
V_B2 = 256
V_ALL = 272
SH1, SC1, GA1, SH2, SC2, GA2 = (NT * i for i in range(6))
C_ID, C_SEL, C_FIX, C_HIST = 0, 128, 128 + SEQS, 128 + SEQS + 64
C_ALL = C_HIST + 4 * NS

def u_hi(t):
    return 8 * (t // KC) + t % KC


POOL_HI, POOL_LO, WIN, CONV_HI, CONV_LO, MIX_LO = 0, 8, 16, 16, 24, 0
Z, XC, BC, CC = 0, 8, 16, 24
YP_HI, YP_LO, MIX_HI, H_LO = 0, 8, 16, 16


def build_layer(nc, a, o):
    with ExitStack() as ctx:
        def sb(name, shape, dt=F32):
            return ctx.enter_context(nc.sbuf_tensor(name, shape, dt))

        def overlay(name, shape, dt, offset):
            return nc.alloc_sbuf_tensor_at(name, shape, dt, offset=offset)

        def here():
            return nc.sbuf_base + (-nc.sbuf_base) % 32

        def sem(name):
            return ctx.enter_context(nc.semaphore(name))

        raw = sb("raw", [P, RAW, US])
        w_hi = sb("w_hi", [P, HL, US], F32R)
        w_lo = sb("w_lo", [P, HL, US], F32R)
        ada_raw = sb("ada_raw", [P, AR, US])
        X = sb("X", [P, NT, TOK])
        at_u = here()
        Uf = sb("Uf", [P, 2 * NT, TOK])
        U = overlay("U", [P, 2 * NT, TOK], F32R, at_u)
        at_p = here()
        PB = sb("PB", [P, 2 * NT, TOK])
        H = overlay("H", [P, 2 * NT, TOK], F32R, at_p)
        G = sb("G", [P, 2 * NT, TOK])
        vec = sb("vec", [P, V_ALL])
        ada = sb("ada", [P, 6 * NT, SEQS])
        c_t = sb("c_t", [P, NT, 32])
        ada_row = sb("ada_row", [P, UC])
        cst = sb("cst", [P, C_ALL])
        hist_sum = sb("hist_sum", [P, PT, NS])
        hist_conv = sb("hist_conv", [P, PT, NS * CH])
        small = sb("small", [P, MT, NS])
        ident = cst[:, C_ID:C_ID + P]
        hist = Uf[:, 24:32, :].rearrange("p t n -> p (t n)")
        zs = PB[:, BC:BC + 4, :].rearrange("p t n -> p (t n)")
        vs = PB[:, BC + 4:BC + 8, :].rearrange("p t n -> p (t n)")
        ones = ada_raw[:, 0, 0:P]
        rstd = ada_raw[:, 1, 0:TOK]
        var_eps = ada_raw[:, 1, TOK:2 * TOK]
        seq_tmp = ada_raw[:, 1, 528:528 + NT * SEQS].rearrange("p (t s) -> p t s", t=NT)
        res_bias = ada_raw[:, 1, 672:672 + NT * SEQS].rearrange("p (t s) -> p t s", t=NT)
        res_scale = ada_raw[:, 1, 816:816 + NT]
        alpha_b = ada_raw[:, 1, 832:832 + NT]

        bank = [ctx.enter_context(nc.psum_tensor(f"main{i}", [P, 512], F32)) for i in range(BANKS)]
        ps_ada = ctx.enter_context(nc.psum_tensor("ps_ada", [P, 512], F32))
        ps_adat = ctx.enter_context(nc.psum_tensor("ps_adat", [P, 512], F32))
        ps_a = ctx.enter_context(nc.psum_tensor("ps_a", [P, 512], F32))
        ps_b = ctx.enter_context(nc.psum_tensor("ps_b", [P, 512], F32))

        raw_landed = [sem(f"raw_landed{i}") for i in range(RAW)]
        ada_landed = [sem(f"ada_landed{i}") for i in range(AR)]
        c_landed, x_landed, vec_landed, hist_landed = (
            sem("c_landed"), sem("x_landed"), sem("vec_landed"), sem("hist_landed"))
        hi_ready = sem("hi_ready")
        unit_split = sem("unit_split")
        part_done = sem("part_done")
        psum_free = sem("psum_free")
        ada_used = sem("ada_used")
        row_copied = sem("row_copied")
        adat_ready = sem("adat_ready")
        ada_ready = sem("ada_ready")
        c_t_psum, c_t_ready = sem("c_t_psum"), sem("c_t_ready")
        vec_psum, vec_ready = sem("vec_psum"), sem("vec_ready")
        hist_psum, hist_ready = sem("hist_psum"), sem("hist_ready")
        x_psum, x_ready = sem("x_psum"), sem("x_ready")
        zeroed = sem("zeroed")
        u_ready = sem("u_ready")
        z_ready, proj_ready = sem("z_ready"), sem("proj_ready")
        z_psum, v_psum, z_staged, v_staged = (
            sem("z_psum"), sem("v_psum"), sem("z_staged"), sem("v_staged"))
        sig_ready, x_scaled = sem("sig_ready"), sem("x_scaled")
        pooled_ready, yp_ready, yc_ready, mixed_ready = (
            sem("pooled_ready"), sem("yp_ready"), sem("yc_ready"), sem("mixed_ready"))
        ln_in, ln_mean, ln_d, ln_sq, ln_var, ln_eps, ln_std, ln_norm = (
            sem("ln_in"), sem("ln_mean"), sem("ln_d"), sem("ln_sq"), sem("ln_var"),
            sem("ln_eps"), sem("ln_std"), sem("ln_norm"))
        u2_ready, res_coef, res_ready = sem("u2_ready"), sem("res_coef"), sem("res_ready")
        r_ready, h_hi_ready, h_ready = sem("r_ready"), sem("h_hi_ready"), sem("h_ready")
        y_ready, y_psum, y_staged = sem("y_ready"), sem("y_psum"), sem("y_staged")
        state_out, stage_out, y_out = sem("state_out"), sem("stage_out"), sem("y_out")

        def rows(w):
            return w.rearrange("(u c p) n -> u p c n", c=KC, p=P)

        w_ada, w_in, w_pu, w_cu, w_o, w_ff1, w_ff2 = (
            rows(a[n][0]) for n in ("w_ada", "w_in", "w_pool_up", "w_conv_up", "w_o", "w_ff1", "w_ff2"))
        w_grp = a["pool_grp_w"][0].rearrange("g (c p) n -> g p c n", p=P)
        raw_u = raw[:, :, :].rearrange("p s (c n) -> p s c n", c=KC)
        hi_u = w_hi[:, :, :].rearrange("p s (c n) -> p s c n", c=KC)
        lo_u = w_lo[:, :, :].rearrange("p s (c n) -> p s c n", c=KC)
        ada_u = ada_raw[:, :, :].rearrange("p s (c n) -> p s c n", c=KC)

        def landed(n):
            return 16 * (n + 1)

        def slot_free(n):
            return n + 1

        def split_slot_free(n):
            return (n + 1) * MT

        def done(n, m=MT - 1):
            return (n + HL) * MT + m + 1

        def split_done(n):
            return RAW + n + 1

        def bank_free(t):
            return t + 1

        block = ctx.enter_context(nc.Block())

        @block.sync
        def _(sp):
            def load_main(s, n, src, size=US):
                sp.wait_ge(unit_split, slot_free(n))
                chunks = size // src.shape[-1]
                dst = raw[:, s, 0:size].rearrange("p (c n) -> p c n", c=chunks)
                sp.dma_start(dst, src).then_inc(raw_landed[s], 16)

            def load_ada(b, u, col):
                s = u % AR
                sp.wait_ge(ada_used, slot_free(ADA_UNITS * b + u))
                sp.dma_start(ada_u[:, s], w_ada[u][:, :, ds(col, UC)]).then_inc(ada_landed[s], 16)

            sp.dma_start(raw[0:SEQS - NS, 3, :], a["c_prompt"]).then_inc(c_landed, 16)
            sp.dma_start(raw[SEQS - NS:SEQS, 3, :], a["c_sample"]).then_inc(c_landed, 16)
            sp.dma_start(cst[:, :], a["cst"]).then_inc(c_landed, 16)
            for u in range(AR):
                load_ada(0, u, 0)
            xp = a["x_prompt"][0].rearrange("(t p) n -> t p n", p=P)
            for t in range(2):
                sp.dma_start(raw[:, t, :], xp[t]).then_inc(x_landed, 16)
            sp.dma_start(raw[0:NS, 2, :], a["x_sample"][:, 0, :]).then_inc(x_landed, 16)
            for u in range(AR, ADA_UNITS):
                load_ada(0, u, 0)
            for u in range(ADA_UNITS):
                load_ada(1, u, D)
            sp.wait_ge(x_psum, NT)
            with sp.Fori(0, 3) as q:
                with sp.Fori(0, 4) as i:
                    n0 = sp.snap(q * 16 + i * 4)
                    for j in range(4):
                        load_ada(q * 4 + i + 2, j, (i * 16 + q * 4 + 4) * P)
                        load_main(j, n0 + j, w_in[ds(q, 1)][0][:, :, ds((i * 4 + j) * UC, UC)])
            with sp.Fori(0, 4) as i:
                for j in range(4):
                    load_ada(i + A_LAST, j, (i * 4 + SC2 + 4) * P)
                    load_main(j, i * 4 + 48 + j, w_in[3][:, :, ds((i * 4 + j) * UC, UC)])
            for g in range(4):
                load_main(g, U_GRP + g, w_grp[g], GW)

            def load_up(n, with_ada):
                for j in range(4):
                    if with_ada:
                        load_ada(n + A_UP, j, (n * NT + GA1) * P)
                    load_main(j, n * 4 + U_UP + j, (w_pu if j < 2 else w_cu)[j % 2][:, :, ds(n * UC, UC)])

            def load_wo(n, with_ada):
                for j in range(4):
                    if with_ada:
                        load_ada(n + A_WO, j, (n * 4 + GA2 + 4) * P)
                    load_main(j, n * 4 + U_WO + j, w_o[j][:, :, ds(n * UC, UC)])

            with sp.Fori(0, 3) as n:
                load_up(n, True)
            load_up(3, False)
            with sp.Fori(0, 3) as n:
                load_wo(n, True)
            load_wo(3, False)
            with sp.Fori(0, 4) as q:
                with sp.Fori(0, 4) as i:
                    for j in range(4):
                        load_main(j, q * 32 + i * 4 + U_FF + j, w_ff1[j][:, :, ds((q * 4 + i) * UC, UC)])
                with sp.Fori(0, 4) as i:
                    for j in range(4):
                        load_main(j, q * 32 + i * 4 + U_FF + 16 + j,
                                  w_ff2[ds(q * 4 + j, 1)][0][:, :, ds(i * UC, UC)])
            yp = o["y_prompt"][0].rearrange("(t p) n -> t p n", p=P)
            for c in range(4):
                cols = slice(c * UC, (c + 1) * UC)
                for t in range(3):
                    sp.wait_ge(y_staged, 3 * c + t + 1)
                    if t < 2:
                        sp.dma_start(yp[t][:, cols], raw[:, t, cols]).then_inc(y_out, 16)
                    else:
                        sp.dma_start(o["y_sample"][:, 0, cols], raw[0:NS, t, cols]).then_inc(y_out, 16)
            sp.wait_ge(y_out, 12 * 16)

        @block.gpsimd
        def _(pool):
            nc.gpsimd.memset(c_t[:, :, :], 0.0).then_inc(zeroed, 1)
            def load_rows(at, rows_, name):
                c, r = divmod(at, P)
                src = a[name][0]
                src = (src.rearrange("k (r n) -> (k r) n", n=P) if len(src.shape) == 2
                       else src.rearrange("(r n) -> r n", n=P))
                pool.dma_start(ada_row[r:r + rows_, c * P:(c + 1) * P], src).then_inc(vec_landed, 16)
            for at, n, name in ((V_BFF1, 64, "b_ff1"), (V_PSCALE, PT, "pool_scale"), (V_CONV, TAPS * PT, "conv_w"),
                                (V_G1, NT, "ln1_g"), (V_B1, NT, "ln1_b"), (V_BADA, 6 * NT, "b_ada"),
                                (V_BFF2, NT, "b_ff2"), (V_G2, NT, "ln2_g"), (V_B2, NT, "ln2_b")):
                load_rows(at, n, name)
            pool.dma_start(hist[0:NS * HIST, 0:PT * P],
                           a["state_pool"][0].rearrange("s h n -> (s h) n")).then_inc(hist_landed, 16)
            pool.dma_start(hist[0:NS * CH, PT * P:2 * PT * P],
                           a["state_conv"][0].rearrange("s h n -> (s h) n")).then_inc(hist_landed, 16)
            nc.gpsimd.memset(PB[:, :, :], 0.0).then_inc(zeroed, 1)
            nc.gpsimd.memset(G[:, :, :], 0.0).then_inc(zeroed, 1)
            pool.dma_start(o["new_pool_sample"][0][:, 0:HIST - 1, :], a["state_pool"][0][:, 1:HIST, :]).then_inc(state_out, 16)
            pool.dma_start(o["new_conv_sample"][0][:, 0:CH - 1, :], a["state_conv"][0][:, 1:CH, :]).then_inc(state_out, 16)

            g_tt, g_ts, g_cp = nc.gpsimd.tensor_tensor, nc.gpsimd.tensor_scalar, nc.gpsimd.tensor_copy
            z8 = PB[:, Z:Z + PT, :]
            A8, B8 = Uf[:, POOL_LO:POOL_LO + PT, :], Uf[:, WIN:WIN + PT, :]
            pool.wait_ge(hist_ready, 1)
            pool.wait_ge(z_ready, 1)

            def window(dst, src, first, step):
                g_tt(dst[:, first:PT, step:PROMPT], src[:, first:PT, step:PROMPT],
                     src[:, first:PT, 0:PROMPT - step], ALU.add)
                g_cp(dst[:, first:PT, 0:step], src[:, first:PT, 0:step])
                pool.drain()

            window(A8, z8, 0, 1)
            window(B8, A8, 2, 2)
            window(A8, B8, 4, 4)
            window(B8, A8, 6, 8)
            sums = [A8[:, 0:2], B8[:, 2:4], A8[:, 4:6], B8[:, 6:8]]
            for g, s in enumerate(sums):
                two = slice(2 * g, 2 * g + 2)
                fix = cst[:, C_FIX + 16 * g:C_FIX + 16 * g + 16].unsqueeze(1).to_broadcast([P, 2, 16])
                g_tt(s[:, :, 0:16], s[:, :, 0:16], fix, ALU.mult)
                g_tt(s[:, :, PROMPT:TOK], PB[:, two, PROMPT:TOK], hist_sum[:, two, :], ALU.add)
            pool.drain()
            for g, s in enumerate(sums):
                g_ts(A8[:, 2 * g:2 * g + 2, :], s, 1.0 / POOL_W[g], None, ALU.mult)
            pool.drain()
            g_tt(A8, A8, z8, ALU.subtract)
            pool.drain()
            g_cp(U[:, POOL_HI:POOL_HI + PT, :], A8)
            pool.drain()
            g_tt(U[:, POOL_LO:POOL_LO + PT, :], A8, U[:, POOL_HI:POOL_HI + PT, :].bitcast(F32),
                 ALU.subtract).then_inc(pooled_ready, 1)

            pool.wait_ge(z_staged, 2)
            pool.dma_start(o["new_pool_prompt"][0][0], zs[0:HIST, 0:PT * P]).then_inc(stage_out, 16)
            pool.dma_start(o["new_pool_sample"][0][:, HIST - 1, :], zs[HIST:HIST + NS, 0:PT * P]).then_inc(stage_out, 16)
            pool.wait_ge(v_staged, 2)
            pool.dma_start(o["new_conv_prompt"][0][0], vs[0:CH, 0:PT * P]).then_inc(stage_out, 16)
            pool.dma_start(o["new_conv_sample"][0][:, CH - 1, :], vs[CH:CH + NS, 0:PT * P]).then_inc(stage_out, 16)
            pool.wait_ge(state_out, 2 * 16)
            pool.wait_ge(stage_out, 4 * 16)

        @block.scalar
        def _(act):
            def hi_part(s, nth, n, size=US):
                act.wait_ge(raw_landed[s], landed(nth))
                act.wait_ge(part_done, split_slot_free(n))
                nc.scalar.activation(w_hi[:, s % HL, 0:size], raw[:, s, 0:size], ACT.Copy).then_inc(hi_ready, 1)

            def copy_row(b, first=False):
                act.wait_ge(ada_used, (b + 1) * ADA_UNITS + AR)
                if first:
                    act.wait_ge(vec_psum, 1)
                else:
                    act.wait_ge(adat_ready, b)
                nc.scalar.copy(ada_row[:, :], ps_ada[:, :]).then_inc(row_copied, 1)

            for t in range(NT):
                act.wait_ge(x_psum, t + 1)
                nc.scalar.copy(X[:, t, :], bank[t % BANKS][:, 0:TOK]).then_inc(x_ready, 1)
            copy_row(0, first=True)
            copy_row(1)
            hi_part(0, 0, 0)
            with act.Fori(0, 3) as q:
                with act.Fori(0, 4) as i:
                    n0 = act.snap(q * 16 + i * 4)
                    b = act.snap(q * 4 + i)
                    for j in range(4):
                        if j == 3:
                            copy_row(b + 2)
                        hi_part((j + 1) % RAW, b + (j + 1) // 4, n0 + (j + 1))
            act.wait_ge(u_ready, 4)
            nc.scalar.mul(X[:, :, :], X[:, :, :], ALPHA).then_inc(x_scaled, 1)
            with act.Fori(0, 3) as i:
                for j in range(4):
                    if j == 3:
                        copy_row(i + A_LAST)
                    hi_part((j + 1) % RAW, i + 12 + (j + 1) // 4, i * 4 + 48 + (j + 1))
            for j in range(4):
                if j == 3:
                    copy_row(A_LAST + 3)
                hi_part((j + 1) % RAW, 15 + (j + 1) // 4, 60 + j + 1, US if j < 3 else GW)
            act.wait_ge(z_psum, 1)
            nc.scalar.copy(zs[0:HIST + NS, 0:512], ps_a[0:HIST + NS, :]).then_inc(z_staged, 1)
            nc.scalar.copy(zs[0:HIST + NS, 512:1024], ps_b[0:HIST + NS, :]).then_inc(z_staged, 1)
            act.wait_ge(v_psum, 1)
            nc.scalar.copy(vs[0:CH + NS, 0:512], bank[0][0:CH + NS, :]).then_inc(v_staged, 1)
            nc.scalar.copy(vs[0:CH + NS, 512:1024], bank[1][0:CH + NS, :]).then_inc(v_staged, 1)
            act.wait_ge(proj_ready, 1)
            for j in range(4):
                hi_part((j + 1) % RAW, 16 + (j + 1) // 4, U_GRP + j + 1, GW if j < 3 else US)
            for g in range(4):
                last = nc.scalar.activation(G[:, 8 * g:8 * g + 8, :], G[:, 8 * g:8 * g + 8, :], ACT.Sigmoid)
            last.then_inc(sig_ready, 1)

            def hi_up(n, with_ada):
                for j in range(4):
                    if j == 3 and with_ada:
                        copy_row(n + A_UP)
                    hi_part((j + 1) % RAW, n + 17 + (j + 1) // 4, n * 4 + U_UP + j + 1)

            def hi_wo(n, with_ada):
                for j in range(4):
                    if j == 3 and with_ada:
                        copy_row(n + A_WO)
                    hi_part((j + 1) % RAW, n + 21 + (j + 1) // 4, n * 4 + U_WO + j + 1)

            with act.Fori(0, 3) as n:
                hi_up(n, True)
            hi_up(3, False)
            with act.Fori(0, 3) as n:
                hi_wo(n, True)
            hi_wo(3, False)

            def norm(l):
                for c in range(4):
                    act.wait_ge(ln_d, 4 * l + c + 1)
                    nc.scalar.activation(G[:, NT + 4 * c:NT + 4 * c + 4, :], G[:, 4 * c:4 * c + 4, :],
                                         ACT.Square).then_inc(ln_sq, 1)
                act.wait_ge(ln_eps, l + 1)
                nc.scalar.activation(rstd, var_eps, ACT.Sqrt).then_inc(ln_std, 1)

            norm(0)
            act.wait_ge(res_coef, 1)
            for t in range(NT):
                act.wait_ge(ln_norm, t // 4 + 1)
                last = nc.scalar.activation(X[:, t, 0:PROMPT], G[:, t, 0:PROMPT], ACT.Identity,
                                            bias=res_bias[:, t, 0:1], scale=res_scale[:, t:t + 1])
            last.then_inc(res_ready, 1)

            def square(b, i):
                act.wait_ge(r_ready, b)
                r = PB[:, H_LO + 4 * i:H_LO + 4 * i + 4, :]
                nc.scalar.activation(r, r, ACT.Square)
                act.drain()
                nc.scalar.copy(H[:, 4 * i:4 * i + 4, :], r).then_inc(h_hi_ready, 1)

            def ff_quarter(q, last=False):
                for i in range(4):
                    for j in range(4):
                        hi_part((j + 1) % RAW, q * 8 + 25 + i + (j + 1) // 4, q * 32 + U_FF + 4 * i + j + 1)
                    square(q * 4 + i + 1, i)
                for i in range(4):
                    for j in range(4):
                        if last and i == 3 and j == 3:
                            continue
                        hi_part((j + 1) % RAW, q * 8 + 29 + i + (j + 1) // 4, q * 32 + U_FF + 16 + 4 * i + j + 1)

            with act.Fori(0, 3) as q:
                ff_quarter(q)
            ff_quarter(3, last=True)
            norm(1)
            for c in range(4):
                for t in range(3):
                    k = 3 * c + t
                    act.wait_ge(y_psum, k + 1)
                    n = P if t < 2 else NS
                    nc.scalar.copy(raw[0:n, t, c * UC:(c + 1) * UC], bank[k % BANKS][0:n, :]).then_inc(y_staged, 1)

        @block.vector
        def _(dve):
            tt, ts, stt, cp = (nc.vector.tensor_tensor, nc.vector.tensor_scalar,
                               nc.vector.scalar_tensor_tensor, nc.vector.tensor_copy)

            def lo_part(s, n, size=US):
                dve.wait_ge(hi_ready, n + 1)
                tt(w_lo[:, s % HL, 0:size], raw[:, s, 0:size], w_hi[:, s % HL, 0:size].bitcast(F32),
                   ALU.subtract).then_inc(unit_split, 1)

            def take_ada(b, tile):
                dve.wait_ge(adat_ready, b + 1)
                src = ps_adat[:, 0:MT * SEQS].rearrange("p (t s) -> p t s", t=MT)
                bias = vec[:, ds(tile + V_BADA, MT)].unsqueeze(2).to_broadcast([P, MT, SEQS])
                tt(ada[:, ds(tile, MT), :], src, bias, ALU.add).then_inc(ada_ready, 1)

            def split(hi, lo, value):
                dve.drain()
                cp(hi, value)
                dve.drain()
                return tt(lo, value, hi.bitcast(F32), ALU.subtract)

            def make_u(q):
                dve.drain()
                for k in range(KC):
                    t = q * KC + k
                    ts(Uf[:, ds(q * 8 + KC + k, 1), 0:PROMPT], X[:, ds(t, 1), 0:PROMPT], ada[:, ds(t + SC1, 1), 0:1].rearrange("p a b -> p (a b)"),
                       ada[:, ds(t + SH1, 1), 0:1].rearrange("p a b -> p (a b)"), ALU.mult, ALU.add)
                t = q * KC
                lo4, hi4 = ds(q * 8 + KC, KC), ds(q * 8, KC)
                s = Uf[:, lo4, PROMPT:TOK]
                tt(s, X[:, ds(t, KC), PROMPT:TOK], ada[:, ds(t + SC1, KC), 1:SEQS], ALU.mult)
                dve.drain()
                tt(s, s, ada[:, ds(t + SH1, KC), 1:SEQS], ALU.add)
                split(U[:, hi4, :], U[:, lo4, :], Uf[:, lo4, :]).then_inc(u_ready, 1)

            dve.sem_inc(unit_split, RAW)
            dve.sem_inc(psum_free, BANKS)
            dve.wait_ge(zeroed, 1)
            dve.wait_ge(c_t_psum, 1)
            cp(c_t[:, :, 0:SEQS], ps_adat[:, 0:NT * SEQS].rearrange("p (t s) -> p t s", t=NT)).then_inc(c_t_ready, 1)
            dve.wait_ge(vec_psum, 1)
            cp(vec[:, :], ps_a[:, 0:V_ALL]).then_inc(vec_ready, 1)
            dve.drain()
            for t in (SC1, SC2):
                v = vec[:, V_BADA + t:V_BADA + t + NT]
                ts(v, v, 1.0, None, ALU.add)
            dve.wait_ge(hist_psum, 1)
            cp(hist_sum[:, :, :], ps_b[:, 0:PT * NS].rearrange("p (t s) -> p t s", t=PT))
            hc = ps_b[:, PT * NS:PT * NS * 3].rearrange("p (t s k) -> p t s k", t=PT, k=CH)
            hd = hist_conv[:, :, :].rearrange("p t (k s) -> p t k s", k=CH)
            for k in range(CH):
                w = vec[:, V_CONV + PT * k:V_CONV + PT * (k + 1)].unsqueeze(2).to_broadcast([P, PT, NS])
                tt(hd[:, :, k], hc[:, :, :, k], w, ALU.mult)
            dve.drain()
            tt(hd[:, :, 0], hd[:, :, 0], hd[:, :, 1], ALU.add).then_inc(hist_ready, 1)
            take_ada(0, 0)
            take_ada(1, SC1)
            dve.wait_ge(x_ready, NT)
            make_u(0)
            dve.wait_ge(zeroed, 3)

            def conv_step(at):
                v, y = PB[:, CC:CC + PT, :], PB[:, XC:XC + PT, :]
                if at == 3:
                    dve.drain().then_inc(z_ready, 1)
                if at == 8:
                    dve.drain()
                    tt(v, v, y, ALU.mult)
                    dve.drain()
                if at == 9:
                    for t in range(PT):
                        w = V_CONV + 2 * PT + t
                        ts(y[:, t, :], v[:, t, :], vec[:, w:w + 1], None, ALU.mult)
                    dve.drain()
                if at in (10, 11):
                    k = 11 - at
                    back = TAPS - 1 - k
                    for t in range(PT):
                        w = V_CONV + PT * k + t
                        stt(y[:, t, back:PROMPT], v[:, t, 0:PROMPT - back], vec[:, w:w + 1],
                            y[:, t, back:PROMPT], ALU.mult, ALU.add)
                    dve.drain()
                if at == 12:
                    tt(y[:, :, PROMPT:TOK], y[:, :, PROMPT:TOK], hd[:, :, 0], ALU.add)
                    dve.drain()
                    tt(y, y, PB[:, BC:BC + PT, :], ALU.mult)

            def in_block(q, i, steady=True):
                for j in range(4):
                    last = not steady and i == 3 and j == 3
                    lo_part((j + 1) % RAW, q * 16 + 4 * i + j + 1, GW if last else US)
                    for m in range(MT):
                        t = 16 * i + 4 * j + m
                        dst = PB[:, t, :] if t < 32 else G[:, t - 32, :]
                        dve.wait_ge(part_done, done(q * 16 + 4 * i + j, m))
                        tt(dst, bank[m][:, 0:TOK], dst, ALU.add).then_inc(psum_free, 1)
                    if steady and i == 2 and j == 1:
                        make_u(q + 1)
                    if not steady:
                        conv_step(4 * i + j)

            lo_part(0, 0)
            with dve.Fori(0, 3) as q:
                for i in range(4):
                    in_block(q, i)
                    take_ada(q * 4 + i + 2, q * 4 + 16 * i + 4)
            for i in range(4):
                in_block(3, i, steady=False)
                take_ada(A_LAST + i, SC2 + 4 + 4 * i)
            dve.drain().then_inc(proj_ready, 1)
            dve.wait_ge(pooled_ready, 1)
            cp(U[:, CONV_HI:CONV_HI + PT, :], PB[:, XC:XC + PT, :])
            dve.drain()
            tt(U[:, CONV_LO:CONV_LO + PT, :], PB[:, XC:XC + PT, :], U[:, CONV_HI:CONV_HI + PT, :].bitcast(F32),
               ALU.subtract).then_inc(yc_ready, 1)
            dve.drain()

            for g in range(4):
                lo_part((g + 1) % RAW, U_GRP + g + 1, GW if g < 3 else US)
                for m in range(2):
                    t = 2 * g + m
                    dve.wait_ge(part_done, done(U_GRP + g, 2 * m + 1))
                    ts(PB[:, YP_LO + t, :], bank[t % BANKS][:, 0:TOK], vec[:, V_PSCALE + t:V_PSCALE + t + 1],
                       None, ALU.mult).then_inc(psum_free, 1)
            split(H[:, YP_HI:YP_HI + PT, :], H[:, YP_LO:YP_LO + PT, :], PB[:, YP_LO:YP_LO + PT, :]).then_inc(yp_ready, 1)

            dve.wait_ge(sig_ready, 1)
            dve.wait_ge(stage_out, 4 * 16)

            def up_block(n, with_ada):
                for j in range(4):
                    lo_part((j + 1) % RAW, n * 4 + U_UP + j + 1)
                    if j % 2 == 0:
                        continue
                    for m in range(MT):
                        dve.wait_ge(part_done, done(n * 4 + U_UP + j, m))
                        g = G[:, ds(n * 4 + NT * (j // 2) + m, 1), :].rearrange("p a n -> p (a n)")
                        tt(g, bank[m][:, 0:TOK], g, ALU.mult).then_inc(psum_free, 1)
                dve.drain()
                lo = Uf[:, ds(n * 4 + MIX_LO, MT), :]
                tt(lo, G[:, ds(n * 4, MT), :], G[:, ds(n * 4 + NT, MT), :], ALU.add)
                split(H[:, ds(n * 4 + MIX_HI, MT), :], U[:, ds(n * 4 + MIX_LO, MT), :], lo).then_inc(mixed_ready, 1)
                if with_ada:
                    take_ada(n + A_UP, n * NT + GA1)

            with dve.Fori(0, 3) as n:
                up_block(n, True)
            up_block(3, False)

            def add_gated(n, x0, gate):
                dve.drain()
                for m in range(MT):
                    dve.wait_ge(part_done, done(n, m))
                    xt = X[:, ds(x0 + m, 1), 0:PROMPT].rearrange("p a n -> p (a n)")
                    gt = ada[:, ds(x0 + gate + m, 1), :].rearrange("p a n -> p (a n)")
                    stt(xt, bank[m][:, 0:PROMPT], gt[:, 0:1], xt, ALU.mult, ALU.add)
                    tt(small[:, m, :], bank[m][:, PROMPT:TOK], gt[:, 1:SEQS], ALU.mult).then_inc(psum_free, 1)
                dve.drain()
                xs = X[:, ds(x0, MT), PROMPT:TOK]
                tt(xs, xs, small[:, :, :], ALU.add)

            dve.wait_ge(x_scaled, 1)
            def wo_block(n, with_ada):
                for j in range(4):
                    lo_part((j + 1) % RAW, n * 4 + U_WO + j + 1)
                add_gated(n * 4 + U_WO + 3, n * 4, GA1)
                if with_ada:
                    take_ada(n + A_WO, n * 4 + GA2 + 4)

            with dve.Fori(0, 3) as n:
                wo_block(n, True)
            wo_block(3, False)

            def norm(l, each):
                if l == 0:
                    nc.vector.memset(ones, 1.0 / D)
                dve.drain().then_inc(ln_in, 1)
                dve.wait_ge(ln_mean, l + 1)
                mu = ps_a[:, 0:TOK].unsqueeze(1).to_broadcast([P, 4, TOK])
                for c in range(4):
                    t4 = slice(4 * c, 4 * c + 4)
                    tt(G[:, t4, :], X[:, t4, :], mu, ALU.subtract).then_inc(ln_d, 1)
                if l == 0:
                    modulation()
                dve.wait_ge(ln_var, l + 1)
                ts(var_eps, ps_b[:, 0:TOK], EPS, None, ALU.add).then_inc(ln_eps, 1)
                dve.wait_ge(ln_std, l + 1)
                nc.vector.reciprocal(rstd, rstd)
                dve.drain()
                r = rstd.unsqueeze(1).to_broadcast([P, 4, TOK])
                for c in range(4):
                    t4 = slice(4 * c, 4 * c + 4)
                    tt(G[:, t4, :], G[:, t4, :], r, ALU.mult).then_inc(ln_norm, 1)
                    dve.drain()
                    each(c)

            def per_seq(col):
                return vec[:, col:col + NT].unsqueeze(2).to_broadcast([P, NT, SEQS])

            def modulation():
                sc2, sh2, ga2 = ada[:, SC2:SC2 + NT, :], ada[:, SH2:SH2 + NT, :], ada[:, GA2:GA2 + NT, :]
                tt(seq_tmp, sc2, per_seq(V_B1), ALU.mult)
                ts(res_scale, vec[:, V_G1:V_G1 + NT], ALPHA, None, ALU.mult)
                ts(alpha_b, vec[:, V_B1:V_B1 + NT], ALPHA, None, ALU.mult)
                tt(res_bias, ga2, per_seq(V_BFF2), ALU.mult)
                dve.drain()
                tt(sh2, sh2, seq_tmp, ALU.add)
                tt(sc2, sc2, per_seq(V_G1), ALU.mult)
                tt(res_bias, res_bias, alpha_b.unsqueeze(2).to_broadcast([P, NT, SEQS]), ALU.add)
                dve.drain().then_inc(res_coef, 1)

            def make_u2(c):
                hi4, lo4 = slice(8 * c, 8 * c + 4), slice(8 * c + 4, 8 * c + 8)
                for k in range(4):
                    t = 4 * c + k
                    ts(Uf[:, 8 * c + 4 + k, 0:PROMPT], G[:, t, 0:PROMPT], ada[:, SC2 + t, 0:1], ada[:, SH2 + t, 0:1],
                       ALU.mult, ALU.add)
                t4 = slice(4 * c, 4 * c + 4)
                s = Uf[:, lo4, PROMPT:TOK]
                xs = X[:, t4, PROMPT:TOK]
                tt(s, G[:, t4, PROMPT:TOK], ada[:, SC2 + 4 * c:SC2 + 4 * c + 4, 1:SEQS], ALU.mult)
                tt(xs, G[:, t4, PROMPT:TOK], res_scale[:, t4].unsqueeze(2).to_broadcast([P, 4, NS]), ALU.mult)
                dve.drain()
                tt(s, s, ada[:, SH2 + 4 * c:SH2 + 4 * c + 4, 1:SEQS], ALU.add)
                tt(xs, xs, res_bias[:, t4, 1:SEQS], ALU.add)
                split(U[:, hi4, :], U[:, lo4, :], Uf[:, lo4, :]).then_inc(u2_ready, 1)

            norm(0, make_u2)

            def lo_h(b, i):
                dve.wait_ge(h_hi_ready, b)
                tt(H[:, H_LO + 4 * i:H_LO + 4 * i + 4, :], PB[:, H_LO + 4 * i:H_LO + 4 * i + 4, :],
                   H[:, 4 * i:4 * i + 4, :].bitcast(F32), ALU.subtract).then_inc(h_ready, 1)

            def ff_quarter(q, last=False):
                for i in range(4):
                    for j in range(4):
                        lo_part((j + 1) % RAW, q * 32 + U_FF + 4 * i + j + 1)
                        if i and j == 0:
                            lo_h(q * 4 + i, i - 1)
                    for m in range(MT):
                        t = 4 * i + m
                        dve.wait_ge(part_done, done(q * 32 + U_FF + 4 * i + 3, m))
                        bias = vec[:, ds(q * 16 + V_BFF1 + t, 1)]
                        r = ts(PB[:, H_LO + t, :], bank[m][:, 0:TOK], bias, 0.0, ALU.add, ALU.max)
                        r.then_inc(psum_free, 1)
                    dve.drain().then_inc(r_ready, 1)
                for i in range(4):
                    for j in range(4):
                        if not (last and i == 3 and j == 3):
                            lo_part((j + 1) % RAW, q * 32 + U_FF + 16 + 4 * i + j + 1)
                        if i == 0 and j == 0:
                            lo_h(q * 4 + 4, 3)
                            dve.wait_ge(res_ready, 1)
                    add_gated(q * 32 + U_FF + 19 + 4 * i, 4 * i, GA2)

            with dve.Fori(0, 3) as q:
                ff_quarter(q)
            ff_quarter(3, last=True)

            def finish(c):
                for k in range(4):
                    t = 4 * c + k
                    r = ts(X[:, t, :], G[:, t, :], vec[:, V_G2 + t:V_G2 + t + 1], vec[:, V_B2 + t:V_B2 + t + 1],
                           ALU.mult, ALU.add)
                r.then_inc(y_ready, 1)

            norm(1, finish)

        @block.tensor
        def _(pe):
            mm = nc.tensor.matmul

            def three(out, w, x_hi, x_lo, start, stop):
                wh, wl = w
                mm(out, wh, x_hi, start=start, stop=False)
                mm(out, wh, x_lo, start=False, stop=False)
                return mm(out, wl, x_hi, start=False, stop=stop)

            def w_of(s, c, m, width=UC):
                cols = slice(c * width + m * P, c * width + (m + 1) * P)
                return w_hi[:, s, cols], w_lo[:, s, cols]

            def tile_of(tensor, t):
                return tensor[:, ds(t, 1), :].rearrange("p a n -> p (a n)")

            def unit(j, n, t0, hi, lo, first=True, last=True):
                pe.wait_ge(unit_split, split_done(n))
                for m in range(MT):
                    if first:
                        pe.wait_ge(psum_free, bank_free(t0 + m))
                    for c in range(KC):
                        r = three(bank[m][:, 0:TOK], w_of(j % HL, c, m), tile_of(hi[0], hi[1] + c),
                                  tile_of(lo[0], lo[1] + c), first and c == 0, last and c == KC - 1)
                    r.then_inc(part_done, 1)

            def ada_unit(b, u, first=False):
                pe.wait_ge(ada_landed[u % AR], (b * 2 + u // AR + 1) * 16)
                if u == 0 and not first:
                    pe.wait_ge(row_copied, b)
                for j in range(KC):
                    r = mm(ps_ada[32 * j:32 * j + 32, :], c_t[:, KC * u + j, :], ada_u[:, u % AR, j, :],
                           start=u == 0, stop=u == ADA_UNITS - 1)
                r.then_inc(ada_used, 1)

            def ada_turn(b, first=False):
                pe.wait_ge(row_copied, b + 1)
                if not first:
                    pe.wait_ge(ada_ready, b)
                for m in range(MT):
                    r = mm(ps_adat[:, SEQS * m:SEQS * (m + 1)], ada_row[:, m * P:(m + 1) * P],
                           cst[:, C_SEL:C_SEL + SEQS], start=True, stop=True)
                r.then_inc(adat_ready, 1)

            pe.sem_inc(part_done, HL * MT)
            pe.sem_inc(ada_used, AR)
            pe.wait_ge(c_landed, 3 * 16)
            for t in range(NT):
                r = mm(ps_adat[:, SEQS * t:SEQS * (t + 1)], raw[0:SEQS, 3, t * P:(t + 1) * P],
                       ident[0:SEQS, 0:SEQS], start=True, stop=True)
            r.then_inc(c_t_psum, 1)
            pe.wait_ge(c_t_ready, 1)
            ada_unit(0, 0, first=True)
            ada_unit(0, 1)
            pe.wait_ge(vec_landed, 9 * 16)
            nc.tensor.transpose(ps_a[:, 0:P], ada_row[:, 0:P], ident)
            nc.tensor.transpose(ps_a[:, P:2 * P], ada_row[:, P:2 * P], ident)
            mm(ps_a[:, V_B2:V_ALL], ada_row[0:NT, 2 * P:3 * P], ident[0:NT, 0:NT], start=True, stop=True).then_inc(vec_psum, 1)
            pe.wait_ge(x_landed, 3 * 16)
            for t in range(NT):
                if t >= BANKS:
                    pe.wait_ge(x_ready, t - BANKS + 1)
                cols = slice(t * P, (t + 1) * P)
                for k in range(2):
                    nc.tensor.transpose(bank[t % BANKS][:, k * P:(k + 1) * P], raw[:, k, cols], ident)
                mm(bank[t % BANKS][:, PROMPT:TOK], raw[0:NS, 2, cols], ident[0:NS, 0:NS], start=True, stop=True).then_inc(x_psum, 1)
            pe.wait_ge(hist_landed, 2 * 16)
            for t in range(PT):
                g = C_HIST + NS * (t // 2)
                mm(ps_b[:, NS * t:NS * (t + 1)], hist[0:NS * HIST, t * P:(t + 1) * P], cst[0:NS * HIST, g:g + NS], start=True, stop=True)
            for t in range(PT):
                c0 = PT * NS + NS * CH * t
                r = mm(ps_b[:, c0:c0 + NS * CH], hist[0:NS * CH, (PT + t) * P:(PT + t + 1) * P],
                       ident[0:NS * CH, 0:NS * CH], start=True, stop=True)
            r.then_inc(hist_psum, 1)
            ada_unit(0, 2)
            ada_unit(0, 3)
            ada_turn(0, first=True)
            for u in range(ADA_UNITS):
                ada_unit(1, u)
            ada_turn(1)

            def in_unit(q, i, j):
                unit(j, q * 16 + i * 4 + j, q * 64 + i * 16 + 4 * j, (U, q * 8), (U, q * 8 + KC))

            with pe.Fori(0, 3) as q:
                with pe.Fori(0, 4) as i:
                    for j in range(4):
                        ada_unit(q * 4 + i + 2, j)
                        pe.wait_ge(u_ready, q + 1)
                        in_unit(q, i, j)
                    ada_turn(q * 4 + i + 2)
            pe.wait_ge(u_ready, 4)
            with pe.Fori(0, 4) as i:
                for j in range(4):
                    ada_unit(i + A_LAST, j)
                    in_unit(3, i, j)
                ada_turn(i + A_LAST)

            pe.wait_ge(proj_ready, 1)
            for t in range(PT):
                b, cols = (ps_a, ps_b)[t // 4], slice(t % 4 * P, t % 4 * P + P)
                r = nc.tensor.transpose(b[0:HIST + NS, cols], PB[:, Z + t, PROMPT - HIST:TOK], ident)
            r.then_inc(z_psum, 1)
            for t in range(PT):
                b, cols = bank[t // 4], slice(t % 4 * P, t % 4 * P + P)
                r = nc.tensor.transpose(b[0:CH + NS, cols], PB[:, CC + t, PROMPT - CH:TOK], ident)
            r.then_inc(v_psum, 1)

            pe.wait_ge(v_staged, 2)
            pe.wait_ge(pooled_ready, 1)
            for g in range(4):
                pe.wait_ge(unit_split, split_done(U_GRP + g))
                for m in range(2):
                    t = 2 * g + m
                    pe.wait_ge(psum_free, bank_free(T_GRP + t))
                    for c in range(2):
                        k = 2 * g + c
                        r = three(bank[t % BANKS][:, 0:TOK], w_of(g % HL, c, m, 2 * P), U[:, POOL_HI + k, :],
                                  U[:, POOL_LO + k, :], c == 0, c == 1)
                    r.then_inc(part_done, MT // 2)

            def up_block(n, with_ada):
                for j in range(4):
                    if with_ada:
                        ada_unit(n + A_UP, j)
                    k = KC * (j % 2)
                    hi, lo = (((H, YP_HI + k), (H, YP_LO + k)), ((U, CONV_HI + k), (U, CONV_LO + k)))[j // 2]
                    unit(j, n * 4 + U_UP + j, n * 8 + T_UP + 4 * (j // 2), hi, lo, j % 2 == 0, j % 2 == 1)
                if with_ada:
                    ada_turn(n + A_UP)

            pe.wait_ge(yp_ready, 1)
            pe.wait_ge(yc_ready, 1)
            with pe.Fori(0, 3) as n:
                up_block(n, True)
            up_block(3, False)

            def wo_block(n, with_ada):
                for j in range(4):
                    if with_ada:
                        ada_unit(n + A_WO, j)
                    pe.wait_ge(mixed_ready, j + 1)
                    unit(j, n * 4 + U_WO + j, n * 4 + T_WO, (H, MIX_HI + KC * j), (U, MIX_LO + KC * j), j == 0, j == 3)
                if with_ada:
                    ada_turn(n + A_WO)

            with pe.Fori(0, 3) as n:
                wo_block(n, True)
            wo_block(3, False)

            def norm(l):
                pe.wait_ge(ln_in, l + 1)
                for t in range(NT):
                    r = mm(ps_a[:, 0:TOK], ones, X[:, t, :], start=t == 0, stop=t == NT - 1)
                r.then_inc(ln_mean, 1)
                for c in range(4):
                    pe.wait_ge(ln_sq, 4 * l + c + 1)
                    for t in range(4 * c, 4 * c + 4):
                        r = mm(ps_b[:, 0:TOK], ones, G[:, NT + t, :], start=t == 0, stop=t == NT - 1)
                r.then_inc(ln_var, 1)

            norm(0)
            with pe.Fori(0, 4) as q:
                with pe.Fori(0, 4) as i:
                    for j in range(4):
                        pe.wait_ge(u2_ready, j + 1)
                        unit(j, q * 32 + i * 4 + U_FF + j, q * 32 + i * 4 + T_FF, (U, 8 * j), (U, 8 * j + KC), j == 0, j == 3)
                with pe.Fori(0, 4) as i:
                    for j in range(4):
                        pe.wait_ge(h_ready, q * 4 + j + 1)
                        unit(j, q * 32 + i * 4 + U_FF + 16 + j, q * 32 + i * 4 + T_FF + 16, (H, KC * j), (H, H_LO + KC * j), j == 0, j == 3)
            norm(1)
            for c in range(4):
                pe.wait_ge(y_ready, c + 1)
                for t in range(3):
                    k = 3 * c + t
                    if k >= BANKS:
                        pe.wait_ge(y_staged, k - BANKS + 1)
                    n, at = (P, t * P) if t < 2 else (NS, PROMPT)
                    for m in range(MT):
                        r = nc.tensor.transpose(bank[k % BANKS][0:n, m * P:(m + 1) * P],
                                                X[:, MT * c + m, at:at + n], ident)
                    r.then_inc(y_psum, 1)


_INS = ["x_prompt", "x_sample", "state_pool", "state_conv", "c_prompt", "c_sample", "w_ada", "b_ada", "w_in",
        "pool_grp_w", "pool_scale", "conv_w", "w_pool_up", "w_conv_up", "w_o", "ln1_g", "ln1_b", "w_ff1", "b_ff1",
        "w_ff2", "b_ff2", "ln2_g", "ln2_b"]
_OUTS = {"y_prompt": (1, PROMPT, D), "y_sample": (NS, 1, D), "new_pool_prompt": (1, 1, HIST, D // 2),
         "new_conv_prompt": (1, 1, CH, D // 2), "new_pool_sample": (1, NS, HIST, D // 2),
         "new_conv_sample": (1, NS, CH, D // 2)}


def constants(np):
    c = np.zeros((P, C_ALL), np.float32)
    c[:, C_ID:C_ID + P] = np.eye(P, dtype=np.float32)
    for g in range(4):
        c[32 * g:32 * g + SEQS, C_SEL:C_SEL + SEQS] = np.eye(SEQS, dtype=np.float32)
    for g, w in enumerate(POOL_W):
        for t in range(16):
            c[:, C_FIX + 16 * g + t] = w / min(w, t + 1)
        for s in range(NS):
            for h in range(HIST - (w - 1), HIST):
                c[s * HIST + h, C_HIST + NS * g + s] = 1.0
    return c


def kernel(**inputs):
    import numpy as _np
    import concourse.bacc as _bacc
    from concourse.bass_utils import run_bass_kernel_spmd as _run

    nc = _bacc.Bacc("TRN2", target_bir_lowering=False, num_devices=1)
    arrays = {f"in_{n}": _np.ascontiguousarray(inputs[n]) for n in _INS}
    arrays["in_cst"] = constants(_np)
    ins = {k[3:]: nc.dram_tensor(k, v.shape, F32, kind="ExternalInput").ap() for k, v in arrays.items()}
    outs = {n: nc.dram_tensor(f"out_{n}", s, F32, kind="ExternalOutput").ap() for n, s in _OUTS.items()}
    build_layer(nc, ins, outs)
    r = _run(nc, [arrays], core_ids=[0]).results[0]
    return tuple(r[f"out_{n}"] for n in _OUTS)
```

```python
from contextlib import ExitStack

import concourse.bass as bass
from concourse import mybir

F32 = mybir.dt.float32
F32R = mybir.dt.float32r
ALU = mybir.AluOpType
ACT = mybir.ActivationFunctionType
ds = bass.ds

P = 128
D = 2048
PROMPT = 256
NS = 8
TOK = PROMPT + NS
SEQS = 1 + NS
NT = D // P
PT = NT // 2
POOL_W = (2, 4, 8, 16)
HIST = max(POOL_W) - 1
CH = 2
TAPS = 3
FF = 4 * D
EPS = 1e-5
ALPHA = 2.0 ** 0.25

KC = 4
UC = 512
MT = UC // P
US = KC * UC
RAW = 4
HL = 2
BANKS = 4
AR = 2
ADA_UNITS = D // P // KC
GW = 512

U_GRP = 64
U_UP = U_GRP + 4
U_WO = U_UP + 16
U_FF = U_WO + 16
T_GRP = 4 * U_GRP
T_UP = T_GRP + PT
T_WO = T_UP + 2 * NT
T_FF = T_WO + NT
A_LAST = 14
A_UP = 18
A_WO = 21

V_BFF1, V_PSCALE, V_CONV, V_G1, V_B1 = 0, 64, 72, 96, 112
V_BADA, V_BFF2, V_G2 = 128, 224, 240
V_B2 = 256
V_ALL = 272
VECTORS = ((V_BFF1, 4 * NT, "b_ff1"), (V_PSCALE, PT, "pool_scale"), (V_CONV, TAPS * PT, "conv_w"),
           (V_G1, NT, "ln1_g"), (V_B1, NT, "ln1_b"), (V_BADA, 6 * NT, "b_ada"),
           (V_BFF2, NT, "b_ff2"), (V_G2, NT, "ln2_g"), (V_B2, NT, "ln2_b"))
SH1, SC1, GA1, SH2, SC2, GA2 = (NT * i for i in range(6))
C_ID, C_SEL, C_FIX, C_HIST = 0, 128, 128 + SEQS, 128 + SEQS + 64
C_ALL = C_HIST + 4 * NS

def u_hi(t):
    return 8 * (t // KC) + t % KC


POOL_HI, POOL_LO, WIN, CONV_HI, CONV_LO, MIX_LO = 0, 8, 16, 16, 24, 0
Z, XC, BC, CC = 0, 8, 16, 24
YP_HI, YP_LO, MIX_HI, H_LO = 0, 8, 16, 16


def build_layer(nc, a, o):
    with ExitStack() as ctx:
        def sb(name, shape, dt=F32):
            return ctx.enter_context(nc.sbuf_tensor(name, shape, dt))

        def overlay(name, shape, dt, offset):
            return nc.alloc_sbuf_tensor_at(name, shape, dt, offset=offset)

        def here():
            return nc.sbuf_base + (-nc.sbuf_base) % 32

        def sem(name):
            return ctx.enter_context(nc.semaphore(name))

        raw = sb("raw", [P, RAW, US])
        w_hi = sb("w_hi", [P, HL, US], F32R)
        w_lo = sb("w_lo", [P, HL, US], F32R)
        ada_raw = sb("ada_raw", [P, AR, US])
        X = sb("X", [P, NT, TOK])
        at_u = here()
        Uf = sb("Uf", [P, 2 * NT, TOK])
        U = overlay("U", [P, 2 * NT, TOK], F32R, at_u)
        at_p = here()
        PB = sb("PB", [P, 2 * NT, TOK])
        H = overlay("H", [P, 2 * NT, TOK], F32R, at_p)
        G = sb("G", [P, 2 * NT, TOK])
        vec = sb("vec", [P, V_ALL])
        ada = sb("ada", [P, 6 * NT, SEQS])
        c_t = sb("c_t", [P, NT, 32])
        ada_row = sb("ada_row", [P, UC])
        cst = sb("cst", [P, C_ALL])
        hist_sum = sb("hist_sum", [P, PT, NS])
        hist_conv = sb("hist_conv", [P, PT, NS * CH])
        small = sb("small", [P, MT, NS])
        ident = cst[:, C_ID:C_ID + P]
        hist = Uf[:, 24:32, :].rearrange("p t n -> p (t n)")
        x_rows = Uf[:, 0:24, :].rearrange("p t n -> p (t n)")[:, 0:3 * D].rearrange("p (k n) -> p k n", k=3)
        first_ada = [w[:, :, :].rearrange("p t n -> p (t n)")[:, 0:ADA_UNITS * US]
                     .rearrange("p (u c n) -> p u c n", u=ADA_UNITS, c=KC) for w in (PB, G)]
        zs = PB[:, BC:BC + 4, :].rearrange("p t n -> p (t n)")
        vs = PB[:, BC + 4:BC + 8, :].rearrange("p t n -> p (t n)")
        ones = hist_conv[:, :, :].rearrange("p t s -> p (t s)")
        rstd = ada_raw[:, 1, 0:TOK]
        var_eps = ada_raw[:, 1, TOK:2 * TOK]
        seq_tmp = ada_raw[:, 1, 528:528 + NT * SEQS].rearrange("p (t s) -> p t s", t=NT)
        res_bias = ada_raw[:, 1, 672:672 + NT * SEQS].rearrange("p (t s) -> p t s", t=NT)
        res_scale = ada_raw[:, 1, 816:816 + NT]
        alpha_b = ada_raw[:, 1, 832:832 + NT]

        bank = [ctx.enter_context(nc.psum_tensor(f"main{i}", [P, 512], F32)) for i in range(BANKS)]
        ps_ada = ctx.enter_context(nc.psum_tensor("ps_ada", [P, 512], F32))
        ps_adat = ctx.enter_context(nc.psum_tensor("ps_adat", [P, 512], F32))
        ps_a = ctx.enter_context(nc.psum_tensor("ps_a", [P, 512], F32))
        ps_b = ctx.enter_context(nc.psum_tensor("ps_b", [P, 512], F32))

        raw_landed = [sem(f"raw_landed{i}") for i in range(RAW)]
        ada_landed = [sem(f"ada_landed{i}") for i in range(AR)]
        first_landed = [sem(f"first_landed{i}") for i in range(2 * ADA_UNITS)]
        c_landed, x_landed, vec_landed, hist_landed = (
            sem("c_landed"), sem("x_landed"), sem("vec_landed"), sem("hist_landed"))
        hi_ready = sem("hi_ready")
        unit_split = sem("unit_split")
        first_rows = sem("first_rows")
        part_done = sem("part_done")
        psum_free = sem("psum_free")
        ada_used = sem("ada_used")
        row_copied = sem("row_copied")
        adat_ready = sem("adat_ready")
        ada_ready = sem("ada_ready")
        c_t_psum, c_t_ready = sem("c_t_psum"), sem("c_t_ready")
        vec_psum, vec_ready = sem("vec_psum"), sem("vec_ready")
        hist_psum, hist_ready = sem("hist_psum"), sem("hist_ready")
        x_psum, x_ready = sem("x_psum"), sem("x_ready")
        zeroed = sem("zeroed")
        u_ready = sem("u_ready")
        z_ready, proj_ready = sem("z_ready"), sem("proj_ready")
        z_psum, v_psum, z_staged, v_staged = (
            sem("z_psum"), sem("v_psum"), sem("z_staged"), sem("v_staged"))
        sig_ready, x_scaled = sem("sig_ready"), sem("x_scaled")
        pooled_ready, yp_ready, yc_ready, mixed_ready = (
            sem("pooled_ready"), sem("yp_ready"), sem("yc_ready"), sem("mixed_ready"))
        avg_ready, ln_in, ln_mean, ln_d, ln_sq, ln_var, ln_eps, ln_std, ln_norm = (
            sem("avg_ready"), sem("ln_in"), sem("ln_mean"), sem("ln_d"), sem("ln_sq"), sem("ln_var"),
            sem("ln_eps"), sem("ln_std"), sem("ln_norm"))
        u2_ready, res_coef, res_ready = sem("u2_ready"), sem("res_coef"), sem("res_ready")
        r_ready, h_hi_ready, h_ready = sem("r_ready"), sem("h_hi_ready"), sem("h_ready")
        y_ready, y_psum, y_staged = sem("y_ready"), sem("y_psum"), sem("y_staged")
        state_out, stage_out, y_out = sem("state_out"), sem("stage_out"), sem("y_out")

        def rows(w):
            return w.rearrange("(u c p) n -> u p c n", c=KC, p=P)

        w_ada, w_in, w_pu, w_cu, w_o, w_ff1, w_ff2 = (
            rows(a[n][0]) for n in ("w_ada", "w_in", "w_pool_up", "w_conv_up", "w_o", "w_ff1", "w_ff2"))
        w_grp = a["pool_grp_w"][0].rearrange("g (c p) n -> g p c n", p=P)
        raw_u = raw[:, :, :].rearrange("p s (c n) -> p s c n", c=KC)
        hi_u = w_hi[:, :, :].rearrange("p s (c n) -> p s c n", c=KC)
        lo_u = w_lo[:, :, :].rearrange("p s (c n) -> p s c n", c=KC)
        ada_u = ada_raw[:, :, :].rearrange("p s (c n) -> p s c n", c=KC)

        def landed(n):
            return 16 * (n + 1)

        def slot_free(n):
            return n + 1

        def split_slot_free(n):
            return (n + 1) * MT

        def done(n, m=MT - 1):
            return (n + HL) * MT + m + 1

        def split_done(n):
            return RAW + n + 1

        def bank_free(t):
            return t + 1

        block = ctx.enter_context(nc.Block())

        @block.sync
        def _(sp):
            def load_main(s, n, src, size=US):
                sp.wait_ge(unit_split, slot_free(n))
                chunks = size // src.shape[-1]
                dst = raw[:, s, 0:size].rearrange("p (c n) -> p c n", c=chunks)
                sp.dma_start(dst, src).then_inc(raw_landed[s], 16)

            def load_ada(b, u, col):
                s = u % AR
                sp.wait_ge(ada_used, slot_free(ADA_UNITS * (b - 2) + u))
                sp.dma_start(ada_u[:, s], w_ada[u][:, :, ds(col, UC)]).then_inc(ada_landed[s], 16)

            def load_rows(at, rows_, name):
                c, r = divmod(at, P)
                src = a[name][0]
                src = (src.rearrange("k (r n) -> (k r) n", n=P) if len(src.shape) == 2
                       else src.rearrange("(r n) -> r n", n=P))
                sp.dma_start(ada_row[r:r + rows_, c * P:(c + 1) * P], src).then_inc(vec_landed, 16)

            sp.dma_start(raw[0:SEQS - NS, 3, :], a["c_prompt"]).then_inc(c_landed, 16)
            sp.dma_start(raw[SEQS - NS:SEQS, 3, :], a["c_sample"]).then_inc(c_landed, 16)
            sp.dma_start(cst[:, :], a["cst"]).then_inc(c_landed, 16)
            for u in range(ADA_UNITS):
                sp.dma_start(first_ada[0][:, u], w_ada[u][:, :, SH1 * P:SH1 * P + UC]).then_inc(first_landed[u], 16)
                for at, n, name in VECTORS[3 * u:3 * u + 3]:
                    load_rows(at, n, name)
            xp = a["x_prompt"][0].rearrange("(t p) n -> t p n", p=P)
            for t in range(2):
                sp.dma_start(x_rows[:, t, :], xp[t]).then_inc(x_landed, 16)
            sp.dma_start(x_rows[0:NS, 2, :], a["x_sample"][:, 0, :]).then_inc(x_landed, 16)
            for u in range(ADA_UNITS):
                sp.dma_start(first_ada[1][:, u], w_ada[u][:, :, SC1 * P:SC1 * P + UC]).then_inc(
                    first_landed[ADA_UNITS + u], 16)
            sp.wait_ge(c_t_psum, 1)
            with sp.Fori(0, 3) as q:
                with sp.Fori(0, 4) as i:
                    n0 = sp.snap(q * 16 + i * 4)
                    for j in range(4):
                        load_main(j, n0 + j, w_in[ds(q, 1)][0][:, :, ds((i * 4 + j) * UC, UC)])
                        load_ada(q * 4 + i + 2, j, (i * 16 + q * 4 + 4) * P)
            with sp.Fori(0, 4) as i:
                for j in range(4):
                    load_main(j, i * 4 + 48 + j, w_in[3][:, :, ds((i * 4 + j) * UC, UC)])
                    load_ada(i + A_LAST, j, (i * 4 + SC2 + 4) * P)
            for g in range(4):
                load_main(g, U_GRP + g, w_grp[g], GW)

            def load_up(n, with_ada):
                for j in range(4):
                    load_main(j, n * 4 + U_UP + j, (w_pu if j < 2 else w_cu)[j % 2][:, :, ds(n * UC, UC)])
                    if with_ada:
                        load_ada(n + A_UP, j, (n * NT + GA1) * P)

            def load_wo(n, with_ada):
                for j in range(4):
                    load_main(j, n * 4 + U_WO + j, w_o[j][:, :, ds(n * UC, UC)])
                    if with_ada:
                        load_ada(n + A_WO, j, (n * 4 + GA2 + 4) * P)

            with sp.Fori(0, 3) as n:
                load_up(n, True)
            load_up(3, False)
            with sp.Fori(0, 3) as n:
                load_wo(n, True)
            load_wo(3, False)
            with sp.Fori(0, 4) as q:
                with sp.Fori(0, 4) as i:
                    for j in range(4):
                        load_main(j, q * 32 + i * 4 + U_FF + j, w_ff1[j][:, :, ds((q * 4 + i) * UC, UC)])
                with sp.Fori(0, 4) as i:
                    for j in range(4):
                        load_main(j, q * 32 + i * 4 + U_FF + 16 + j,
                                  w_ff2[ds(q * 4 + j, 1)][0][:, :, ds(i * UC, UC)])
            yp = o["y_prompt"][0].rearrange("(t p) n -> t p n", p=P)
            for c in range(4):
                cols = slice(c * UC, (c + 1) * UC)
                for t in range(3):
                    sp.wait_ge(y_staged, 3 * c + t + 1)
                    if t < 2:
                        sp.dma_start(yp[t][:, cols], raw[:, t, cols]).then_inc(y_out, 16)
                    else:
                        sp.dma_start(o["y_sample"][:, 0, cols], raw[0:NS, t, cols]).then_inc(y_out, 16)
            sp.wait_ge(y_out, 12 * 16)

        @block.gpsimd
        def _(pool):
            nc.gpsimd.memset(c_t[:, :, :], 0.0).then_inc(zeroed, 1)
            pool.dma_start(hist[0:NS * HIST, 0:PT * P],
                           a["state_pool"][0].rearrange("s h n -> (s h) n")).then_inc(hist_landed, 16)
            pool.dma_start(hist[0:NS * CH, PT * P:2 * PT * P],
                           a["state_conv"][0].rearrange("s h n -> (s h) n")).then_inc(hist_landed, 16)
            pool.dma_start(o["new_pool_sample"][0][:, 0:HIST - 1, :], a["state_pool"][0][:, 1:HIST, :]).then_inc(state_out, 16)
            pool.dma_start(o["new_conv_sample"][0][:, 0:CH - 1, :], a["state_conv"][0][:, 1:CH, :]).then_inc(state_out, 16)

            g_tt, g_ts, g_cp = nc.gpsimd.tensor_tensor, nc.gpsimd.tensor_scalar, nc.gpsimd.tensor_copy
            z8 = PB[:, Z:Z + PT, :]
            A8, B8 = Uf[:, POOL_LO:POOL_LO + PT, :], Uf[:, WIN:WIN + PT, :]
            pool.wait_ge(hist_ready, 1)
            pool.wait_ge(z_ready, 1)

            def window(dst, src, first, step):
                g_tt(dst[:, first:PT, step:PROMPT], src[:, first:PT, step:PROMPT],
                     src[:, first:PT, 0:PROMPT - step], ALU.add)
                g_cp(dst[:, first:PT, 0:step], src[:, first:PT, 0:step])
                pool.drain()

            window(A8, z8, 0, 1)
            window(B8, A8, 2, 2)
            window(A8, B8, 4, 4)
            window(B8, A8, 6, 8)
            sums = [A8[:, 0:2], B8[:, 2:4], A8[:, 4:6], B8[:, 6:8]]
            for g, s in enumerate(sums):
                two = slice(2 * g, 2 * g + 2)
                fix = cst[:, C_FIX + 16 * g:C_FIX + 16 * g + 16].unsqueeze(1).to_broadcast([P, 2, 16])
                g_tt(s[:, :, 0:16], s[:, :, 0:16], fix, ALU.mult)
                g_tt(s[:, :, PROMPT:TOK], PB[:, two, PROMPT:TOK], hist_sum[:, two, :], ALU.add)
            pool.drain()
            for g, s in enumerate(sums):
                g_ts(A8[:, 2 * g:2 * g + 2, :], s, 1.0 / POOL_W[g], None, ALU.mult)
            pool.drain()
            g_tt(A8, A8, z8, ALU.subtract)
            pool.drain()
            g_cp(U[:, POOL_HI:POOL_HI + PT, :], A8)
            pool.drain()
            g_tt(U[:, POOL_LO:POOL_LO + PT, :], A8, U[:, POOL_HI:POOL_HI + PT, :].bitcast(F32),
                 ALU.subtract).then_inc(pooled_ready, 1)

            pool.wait_ge(z_staged, 2)
            pool.dma_start(o["new_pool_prompt"][0][0], zs[0:HIST, 0:PT * P]).then_inc(stage_out, 16)
            pool.dma_start(o["new_pool_sample"][0][:, HIST - 1, :], zs[HIST:HIST + NS, 0:PT * P]).then_inc(stage_out, 16)
            pool.wait_ge(v_staged, 2)
            pool.dma_start(o["new_conv_prompt"][0][0], vs[0:CH, 0:PT * P]).then_inc(stage_out, 16)
            pool.dma_start(o["new_conv_sample"][0][:, CH - 1, :], vs[CH:CH + NS, 0:PT * P]).then_inc(stage_out, 16)
            pool.wait_ge(state_out, 2 * 16)
            pool.wait_ge(stage_out, 4 * 16)

        @block.scalar
        def _(act):
            def hi_part(s, nth, n, size=US):
                act.wait_ge(raw_landed[s], landed(nth))
                act.wait_ge(part_done, split_slot_free(n))
                nc.scalar.activation(w_hi[:, s % HL, 0:size], raw[:, s, 0:size], ACT.Copy).then_inc(hi_ready, 1)

            def copy_row(b):
                if isinstance(b, int) and b < 2:
                    act.wait_ge(first_rows, b + 1)
                else:
                    act.wait_ge(ada_used, (b - 1) * ADA_UNITS + AR)
                if isinstance(b, int) and b == 0:
                    act.wait_ge(vec_psum, 1)
                else:
                    act.wait_ge(adat_ready, b)
                nc.scalar.copy(ada_row[:, :], ps_ada[:, :]).then_inc(row_copied, 1)

            copy_row(0)
            for t in range(NT):
                act.wait_ge(x_psum, t + 1)
                nc.scalar.copy(X[:, t, :], bank[t % BANKS][:, 0:TOK]).then_inc(x_ready, 1)
            copy_row(1)
            hi_part(0, 0, 0)
            with act.Fori(0, 3) as q:
                with act.Fori(0, 4) as i:
                    n0 = act.snap(q * 16 + i * 4)
                    b = act.snap(q * 4 + i)
                    for j in range(4):
                        if j == 3:
                            copy_row(b + 2)
                        hi_part((j + 1) % RAW, b + (j + 1) // 4, n0 + (j + 1))
            act.wait_ge(u_ready, 4)
            nc.scalar.mul(X[:, :, :], X[:, :, :], ALPHA).then_inc(x_scaled, 1)
            with act.Fori(0, 3) as i:
                for j in range(4):
                    if j == 3:
                        copy_row(i + A_LAST)
                    hi_part((j + 1) % RAW, i + 12 + (j + 1) // 4, i * 4 + 48 + (j + 1))
            for j in range(4):
                if j == 3:
                    copy_row(A_LAST + 3)
                hi_part((j + 1) % RAW, 15 + (j + 1) // 4, 60 + j + 1, US if j < 3 else GW)
            act.wait_ge(z_psum, 1)
            nc.scalar.copy(zs[0:HIST + NS, 0:512], ps_a[0:HIST + NS, :]).then_inc(z_staged, 1)
            nc.scalar.copy(zs[0:HIST + NS, 512:1024], ps_b[0:HIST + NS, :]).then_inc(z_staged, 1)
            act.wait_ge(v_psum, 1)
            nc.scalar.copy(vs[0:CH + NS, 0:512], ps_ada[0:CH + NS, :]).then_inc(v_staged, 1)
            nc.scalar.copy(vs[0:CH + NS, 512:1024], ps_adat[0:CH + NS, :]).then_inc(v_staged, 1)
            act.wait_ge(proj_ready, 1)
            for j in range(4):
                hi_part((j + 1) % RAW, 16 + (j + 1) // 4, U_GRP + j + 1, GW if j < 3 else US)
            for g in range(4):
                last = nc.scalar.activation(G[:, 8 * g:8 * g + 8, :], G[:, 8 * g:8 * g + 8, :], ACT.Sigmoid)
            last.then_inc(sig_ready, 1)

            def hi_up(n, with_ada):
                for j in range(4):
                    if j == 3 and with_ada:
                        copy_row(n + A_UP)
                    hi_part((j + 1) % RAW, n + 17 + (j + 1) // 4, n * 4 + U_UP + j + 1)

            def hi_wo(n, with_ada):
                for j in range(4):
                    if j == 3 and with_ada:
                        copy_row(n + A_WO)
                    hi_part((j + 1) % RAW, n + 21 + (j + 1) // 4, n * 4 + U_WO + j + 1)

            with act.Fori(0, 3) as n:
                hi_up(n, True)
            hi_up(3, False)
            with act.Fori(0, 3) as n:
                hi_wo(n, True)
            hi_wo(3, False)

            def norm(l):
                for c in range(4):
                    act.wait_ge(ln_d, 4 * l + c + 1)
                    nc.scalar.activation(G[:, NT + 4 * c:NT + 4 * c + 4, :], G[:, 4 * c:4 * c + 4, :],
                                         ACT.Square).then_inc(ln_sq, 1)
                nc.scalar.activation(rstd[:, 0:1], ones[:, 0:1], ACT.Sqrt)
                act.drain()
                act.wait_ge(ln_eps, l + 1)
                nc.scalar.activation(rstd, var_eps, ACT.Sqrt).then_inc(ln_std, 1)

            norm(0)
            act.wait_ge(res_coef, 1)
            for t in range(NT):
                act.wait_ge(ln_norm, t // 4 + 1)
                last = nc.scalar.activation(X[:, t, 0:PROMPT], G[:, t, 0:PROMPT], ACT.Identity,
                                            bias=res_bias[:, t, 0:1], scale=res_scale[:, t:t + 1])
            last.then_inc(res_ready, 1)

            def square(b, i):
                act.wait_ge(r_ready, b)
                r = PB[:, H_LO + 4 * i:H_LO + 4 * i + 4, :]
                nc.scalar.activation(r, r, ACT.Square)
                act.drain()
                nc.scalar.copy(H[:, 4 * i:4 * i + 4, :], r).then_inc(h_hi_ready, 1)

            def ff_quarter(q, last=False):
                for i in range(4):
                    for j in range(4):
                        hi_part((j + 1) % RAW, q * 8 + 25 + i + (j + 1) // 4, q * 32 + U_FF + 4 * i + j + 1)
                        if i and j == 0:
                            square(q * 4 + i, i - 1)
                for i in range(4):
                    for j in range(4):
                        if last and i == 3 and j == 3:
                            continue
                        hi_part((j + 1) % RAW, q * 8 + 29 + i + (j + 1) // 4, q * 32 + U_FF + 16 + 4 * i + j + 1)
                        if i == 0 and j == 0:
                            square(q * 4 + 4, 3)

            with act.Fori(0, 3) as q:
                ff_quarter(q)
            ff_quarter(3, last=True)
            norm(1)
            for c in range(4):
                act.wait_ge(ln_norm, 4 + c + 1)
                for t in range(4 * c, 4 * c + 4):
                    last = nc.scalar.activation(X[:, t, :], G[:, t, :], ACT.Identity,
                                                bias=vec[:, V_B2 + t:V_B2 + t + 1], scale=vec[:, V_G2 + t:V_G2 + t + 1])
                last.then_inc(y_ready, 1)
            for c in range(4):
                for t in range(3):
                    k = 3 * c + t
                    act.wait_ge(y_psum, k + 1)
                    n = P if t < 2 else NS
                    nc.scalar.copy(raw[0:n, t, c * UC:(c + 1) * UC], bank[k % BANKS][0:n, :]).then_inc(y_staged, 1)

        @block.vector
        def _(dve):
            tt, ts, stt, cp = (nc.vector.tensor_tensor, nc.vector.tensor_scalar,
                               nc.vector.scalar_tensor_tensor, nc.vector.tensor_copy)

            def lo_part(s, n, size=US):
                dve.wait_ge(hi_ready, n + 1)
                tt(w_lo[:, s % HL, 0:size], raw[:, s, 0:size], w_hi[:, s % HL, 0:size].bitcast(F32),
                   ALU.subtract).then_inc(unit_split, 1)

            def take_ada(b, tile):
                dve.wait_ge(adat_ready, b + 1)
                src = ps_adat[:, 0:MT * SEQS].rearrange("p (t s) -> p t s", t=MT)
                bias = vec[:, ds(tile + V_BADA, MT)].unsqueeze(2).to_broadcast([P, MT, SEQS])
                tt(ada[:, ds(tile, MT), :], src, bias, ALU.add).then_inc(ada_ready, 1)

            def split(hi, lo, value):
                dve.drain()
                cp(hi, value)
                dve.drain()
                return tt(lo, value, hi.bitcast(F32), ALU.subtract)

            def make_u(q):
                dve.drain()
                for k in range(KC):
                    t = q * KC + k
                    ts(Uf[:, ds(q * 8 + KC + k, 1), 0:PROMPT], X[:, ds(t, 1), 0:PROMPT], ada[:, ds(t + SC1, 1), 0:1].rearrange("p a b -> p (a b)"),
                       ada[:, ds(t + SH1, 1), 0:1].rearrange("p a b -> p (a b)"), ALU.mult, ALU.add)
                t = q * KC
                lo4 = ds(q * 8 + KC, KC)
                s = Uf[:, lo4, PROMPT:TOK]
                tt(s, X[:, ds(t, KC), PROMPT:TOK], ada[:, ds(t + SC1, KC), 1:SEQS], ALU.mult)
                dve.drain()
                tt(s, s, ada[:, ds(t + SH1, KC), 1:SEQS], ALU.add)

            def split_u(q):
                hi4, lo4 = ds(q * 8, KC), ds(q * 8 + KC, KC)
                split(U[:, hi4, :], U[:, lo4, :], Uf[:, lo4, :]).then_inc(u_ready, 1)

            dve.sem_inc(unit_split, RAW)
            dve.sem_inc(psum_free, BANKS)
            dve.wait_ge(zeroed, 1)
            dve.wait_ge(c_t_psum, 1)
            cp(c_t[:, :, 0:SEQS], ps_adat[:, 0:NT * SEQS].rearrange("p (t s) -> p t s", t=NT)).then_inc(c_t_ready, 1)
            dve.wait_ge(vec_psum, 1)
            cp(vec[:, :], ps_a[:, 0:V_ALL]).then_inc(vec_ready, 1)
            dve.drain()
            for t in (SC1, SC2):
                v = vec[:, V_BADA + t:V_BADA + t + NT]
                ts(v, v, 1.0, None, ALU.add)
            dve.drain()
            take_ada(0, SH1)
            dve.wait_ge(x_ready, NT)
            take_ada(1, SC1)
            make_u(0)
            split_u(0)
            lo_part(0, 0)
            dve.wait_ge(hist_psum, 1)
            cp(hist_sum[:, :, :], ps_b[:, 0:PT * NS].rearrange("p (t s) -> p t s", t=PT))
            hc = ps_b[:, PT * NS:PT * NS * 3].rearrange("p (t s k) -> p t s k", t=PT, k=CH)
            hd = hist_conv[:, :, :].rearrange("p t (k s) -> p t k s", k=CH)
            for k in range(CH):
                w = vec[:, V_CONV + PT * k:V_CONV + PT * (k + 1)].unsqueeze(2).to_broadcast([P, PT, NS])
                tt(hd[:, :, k], hc[:, :, :, k], w, ALU.mult)
            dve.drain()
            tt(hd[:, :, 0], hd[:, :, 0], hd[:, :, 1], ALU.add).then_inc(hist_ready, 1)

            def conv_step(at):
                v, y = PB[:, CC:CC + PT, :], PB[:, XC:XC + PT, :]
                if at == 3:
                    dve.drain().then_inc(z_ready, 1)
                if at == 8:
                    dve.drain()
                    tt(v, v, y, ALU.mult)
                    dve.drain()
                if at == 9:
                    for t in range(PT):
                        w = V_CONV + 2 * PT + t
                        ts(y[:, t, :], v[:, t, :], vec[:, w:w + 1], None, ALU.mult)
                    dve.drain()
                if at in (10, 11):
                    k = 11 - at
                    back = TAPS - 1 - k
                    for t in range(PT):
                        w = V_CONV + PT * k + t
                        stt(y[:, t, back:PROMPT], v[:, t, 0:PROMPT - back], vec[:, w:w + 1],
                            y[:, t, back:PROMPT], ALU.mult, ALU.add)
                    dve.drain()
                if at == 12:
                    tt(y[:, :, PROMPT:TOK], y[:, :, PROMPT:TOK], hd[:, :, 0], ALU.add)
                    dve.drain()
                    tt(y, y, PB[:, BC:BC + PT, :], ALU.mult)

            def in_block(q, i, steady=True, first=False):
                for j in range(4):
                    last = not steady and i == 3 and j == 3
                    lo_part((j + 1) % RAW, q * 16 + 4 * i + j + 1, GW if last else US)
                    for m in range(MT):
                        t = 16 * i + 4 * j + m
                        dst = PB[:, t, :] if t < 32 else G[:, t - 32, :]
                        dve.wait_ge(part_done, done(q * 16 + 4 * i + j, m))
                        if first:
                            cp(dst, bank[m][:, 0:TOK]).then_inc(psum_free, 1)
                        else:
                            tt(dst, bank[m][:, 0:TOK], dst, ALU.add).then_inc(psum_free, 1)
                    if steady and i == 2 and j == 1:
                        make_u(q + 1)
                    if steady and i == 2 and j == 2:
                        split_u(q + 1)
                    if not steady:
                        conv_step(4 * i + j)

            for i in range(4):
                in_block(0, i, first=True)
                take_ada(i + 2, 16 * i + 4)
            with dve.Fori(1, 3) as q:
                for i in range(4):
                    in_block(q, i)
                    take_ada(q * 4 + i + 2, q * 4 + 16 * i + 4)
            for i in range(4):
                in_block(3, i, steady=False)
                take_ada(A_LAST + i, SC2 + 4 + 4 * i)
            dve.drain().then_inc(proj_ready, 1)
            dve.wait_ge(pooled_ready, 1)
            conv = PB[:, XC:XC + PT, :]
            cp(U[:, CONV_HI:CONV_HI + PT, :], conv)
            lo_part(1, U_GRP + 1, GW)
            dve.drain()
            tt(U[:, CONV_LO:CONV_LO + PT, :], conv, U[:, CONV_HI:CONV_HI + PT, :].bitcast(F32),
               ALU.subtract).then_inc(yc_ready, 1)
            dve.drain()

            for g in range(4):
                if g:
                    lo_part((g + 1) % RAW, U_GRP + g + 1, GW if g < 3 else US)
                for m in range(2):
                    t = 2 * g + m
                    dve.wait_ge(part_done, done(U_GRP + g, 2 * m + 1))
                    ts(PB[:, YP_LO + t, :], bank[t % BANKS][:, 0:TOK], vec[:, V_PSCALE + t:V_PSCALE + t + 1],
                       None, ALU.mult).then_inc(psum_free, 1)
                if g % 2:
                    a4, b4 = 2 * g - 2, 2 * g + 2
                    split(H[:, YP_HI + a4:YP_HI + b4, :], H[:, YP_LO + a4:YP_LO + b4, :],
                          PB[:, YP_LO + a4:YP_LO + b4, :]).then_inc(yp_ready, 1)

            dve.wait_ge(sig_ready, 1)
            dve.wait_ge(stage_out, 4 * 16)

            def up_block(n, with_ada):
                for j in range(4):
                    lo_part((j + 1) % RAW, n * 4 + U_UP + j + 1)
                    if j % 2 == 0:
                        continue
                    for m in range(MT):
                        dve.wait_ge(part_done, done(n * 4 + U_UP + j, m))
                        g = G[:, ds(n * 4 + NT * (j // 2) + m, 1), :].rearrange("p a n -> p (a n)")
                        tt(g, bank[m][:, 0:TOK], g, ALU.mult).then_inc(psum_free, 1)
                dve.drain()
                lo = Uf[:, ds(n * 4 + MIX_LO, MT), :]
                tt(lo, G[:, ds(n * 4, MT), :], G[:, ds(n * 4 + NT, MT), :], ALU.add)
                split(H[:, ds(n * 4 + MIX_HI, MT), :], U[:, ds(n * 4 + MIX_LO, MT), :], lo).then_inc(mixed_ready, 1)
                if with_ada:
                    take_ada(n + A_UP, n * NT + GA1)

            with dve.Fori(0, 3) as n:
                up_block(n, True)
            up_block(3, False)

            def add_gated(n, x0, gate, final=True):
                dve.drain()
                for m in range(MT):
                    dve.wait_ge(part_done, done(n, m))
                    xt = X[:, ds(x0 + m, 1), 0:PROMPT].rearrange("p a n -> p (a n)")
                    gt = ada[:, ds(x0 + gate + m, 1), :].rearrange("p a n -> p (a n)")
                    stt(xt, bank[m][:, 0:PROMPT], gt[:, 0:1], xt, ALU.mult, ALU.add)
                    tt(small[:, m, :], bank[m][:, PROMPT:TOK], gt[:, 1:SEQS], ALU.mult).then_inc(psum_free, 1)
                dve.drain()
                xs = X[:, ds(x0, MT), PROMPT:TOK]
                r = tt(xs, xs, small[:, :, :], ALU.add)
                if final:
                    r.then_inc(ln_in, 1)

            dve.wait_ge(x_scaled, 1)
            nc.vector.memset(ones, 1.0 / D).then_inc(avg_ready, 1)
            def wo_block(n, with_ada):
                for j in range(4):
                    lo_part((j + 1) % RAW, n * 4 + U_WO + j + 1)
                add_gated(n * 4 + U_WO + 3, n * 4, GA1)
                if with_ada:
                    take_ada(n + A_WO, n * 4 + GA2 + 4)

            with dve.Fori(0, 3) as n:
                wo_block(n, True)
            wo_block(3, False)

            def norm(l, each):
                dve.wait_ge(ln_mean, l + 1)
                mu = ps_a[:, 0:TOK].unsqueeze(1).to_broadcast([P, 4, TOK])
                for c in range(4):
                    t4 = slice(4 * c, 4 * c + 4)
                    tt(G[:, t4, :], X[:, t4, :], mu, ALU.subtract).then_inc(ln_d, 1)
                if l == 0:
                    modulation()
                dve.wait_ge(ln_var, l + 1)
                ts(var_eps, ps_b[:, 0:TOK], EPS, None, ALU.add).then_inc(ln_eps, 1)
                dve.wait_ge(ln_std, l + 1)
                nc.vector.reciprocal(rstd, rstd)
                dve.drain()
                r = rstd.unsqueeze(1).to_broadcast([P, 4, TOK])
                for c in range(4):
                    t4 = slice(4 * c, 4 * c + 4)
                    tt(G[:, t4, :], G[:, t4, :], r, ALU.mult).then_inc(ln_norm, 1)
                    dve.drain()
                    each(c)

            def per_seq(col):
                return vec[:, col:col + NT].unsqueeze(2).to_broadcast([P, NT, SEQS])

            def modulation():
                sc2, sh2, ga2 = ada[:, SC2:SC2 + NT, :], ada[:, SH2:SH2 + NT, :], ada[:, GA2:GA2 + NT, :]
                tt(seq_tmp, sc2, per_seq(V_B1), ALU.mult)
                ts(res_scale, vec[:, V_G1:V_G1 + NT], ALPHA, None, ALU.mult)
                ts(alpha_b, vec[:, V_B1:V_B1 + NT], ALPHA, None, ALU.mult)
                tt(res_bias, ga2, per_seq(V_BFF2), ALU.mult)
                dve.drain()
                tt(sh2, sh2, seq_tmp, ALU.add)
                tt(sc2, sc2, per_seq(V_G1), ALU.mult)
                tt(res_bias, res_bias, alpha_b.unsqueeze(2).to_broadcast([P, NT, SEQS]), ALU.add)
                dve.drain().then_inc(res_coef, 1)

            def make_u2(c):
                hi4, lo4 = slice(8 * c, 8 * c + 4), slice(8 * c + 4, 8 * c + 8)
                for k in range(4):
                    t = 4 * c + k
                    ts(Uf[:, 8 * c + 4 + k, 0:PROMPT], G[:, t, 0:PROMPT], ada[:, SC2 + t, 0:1], ada[:, SH2 + t, 0:1],
                       ALU.mult, ALU.add)
                t4 = slice(4 * c, 4 * c + 4)
                s = Uf[:, lo4, PROMPT:TOK]
                xs = X[:, t4, PROMPT:TOK]
                tt(s, G[:, t4, PROMPT:TOK], ada[:, SC2 + 4 * c:SC2 + 4 * c + 4, 1:SEQS], ALU.mult)
                tt(xs, G[:, t4, PROMPT:TOK], res_scale[:, t4].unsqueeze(2).to_broadcast([P, 4, NS]), ALU.mult)
                dve.drain()
                tt(s, s, ada[:, SH2 + 4 * c:SH2 + 4 * c + 4, 1:SEQS], ALU.add)
                tt(xs, xs, res_bias[:, t4, 1:SEQS], ALU.add)
                split(U[:, hi4, :], U[:, lo4, :], Uf[:, lo4, :]).then_inc(u2_ready, 1)

            norm(0, make_u2)

            def lo_h(b, i):
                dve.wait_ge(h_hi_ready, b)
                tt(H[:, H_LO + 4 * i:H_LO + 4 * i + 4, :], PB[:, H_LO + 4 * i:H_LO + 4 * i + 4, :],
                   H[:, 4 * i:4 * i + 4, :].bitcast(F32), ALU.subtract).then_inc(h_ready, 1)

            def ff_quarter(q, last=False):
                for i in range(4):
                    for j in range(4):
                        lo_part((j + 1) % RAW, q * 32 + U_FF + 4 * i + j + 1)
                        if i and j == 0:
                            lo_h(q * 4 + i, i - 1)
                    for m in range(MT):
                        t = 4 * i + m
                        dve.wait_ge(part_done, done(q * 32 + U_FF + 4 * i + 3, m))
                        bias = vec[:, ds(q * 16 + V_BFF1 + t, 1)]
                        r = ts(PB[:, H_LO + t, :], bank[m][:, 0:TOK], bias, 0.0, ALU.add, ALU.max)
                        r.then_inc(psum_free, 1)
                    dve.drain().then_inc(r_ready, 1)
                for i in range(4):
                    for j in range(4):
                        if not (last and i == 3 and j == 3):
                            lo_part((j + 1) % RAW, q * 32 + U_FF + 16 + 4 * i + j + 1)
                        if i == 0 and j == 0:
                            lo_h(q * 4 + 4, 3)
                            dve.wait_ge(res_ready, 1)
                    add_gated(q * 32 + U_FF + 19 + 4 * i, 4 * i, GA2, final=last)

            with dve.Fori(0, 3) as q:
                ff_quarter(q)
            ff_quarter(3, last=True)

            norm(1, lambda c: None)

        @block.tensor
        def _(pe):
            mm = nc.tensor.matmul

            def three(out, w, x_hi, x_lo, start, stop):
                wh, wl = w
                mm(out, wh, x_hi, start=start, stop=False)
                mm(out, wh, x_lo, start=False, stop=False)
                return mm(out, wl, x_hi, start=False, stop=stop)

            def w_of(s, c, m, width=UC):
                cols = slice(c * width + m * P, c * width + (m + 1) * P)
                return w_hi[:, s, cols], w_lo[:, s, cols]

            def tile_of(tensor, t):
                return tensor[:, ds(t, 1), :].rearrange("p a n -> p (a n)")

            def unit(j, n, t0, hi, lo, first=True, last=True):
                pe.wait_ge(unit_split, split_done(n))
                for m in range(MT):
                    if first:
                        pe.wait_ge(psum_free, bank_free(t0 + m))
                    for c in range(KC):
                        r = three(bank[m][:, 0:TOK], w_of(j % HL, c, m), tile_of(hi[0], hi[1] + c),
                                  tile_of(lo[0], lo[1] + c), first and c == 0, last and c == KC - 1)
                    r.then_inc(part_done, 1)

            def four_chunks(u, w):
                for j in range(KC):
                    r = mm(ps_ada[32 * j:32 * j + 32, :], c_t[:, KC * u + j, :], w[:, j, :],
                           start=u == 0, stop=u == ADA_UNITS - 1)
                return r

            def first_block(b):
                if b:
                    pe.wait_ge(row_copied, b)
                for u in range(ADA_UNITS):
                    pe.wait_ge(first_landed[ADA_UNITS * b + u], 16)
                    r = four_chunks(u, first_ada[b][:, u])
                r.then_inc(first_rows, 1)

            def ada_unit(b, u):
                pe.wait_ge(ada_landed[u % AR], ((b - 2) * 2 + u // AR + 1) * 16)
                if u == 0:
                    pe.wait_ge(row_copied, b)
                four_chunks(u, ada_u[:, u % AR]).then_inc(ada_used, 1)

            def ada_turn(b, first=False):
                pe.wait_ge(row_copied, b + 1)
                if not first:
                    pe.wait_ge(ada_ready, b)
                for m in range(MT):
                    r = mm(ps_adat[:, SEQS * m:SEQS * (m + 1)], ada_row[:, m * P:(m + 1) * P],
                           cst[:, C_SEL:C_SEL + SEQS], start=True, stop=True)
                r.then_inc(adat_ready, 1)

            pe.sem_inc(part_done, HL * MT)
            pe.sem_inc(ada_used, AR)
            pe.wait_ge(c_landed, 3 * 16)
            for t in range(NT):
                r = nc.tensor.transpose(ps_adat[:, SEQS * t:SEQS * (t + 1)], raw[0:SEQS, 3, t * P:(t + 1) * P],
                                        ident[0:SEQS, 0:SEQS])
            r.then_inc(c_t_psum, 1)
            pe.wait_ge(c_t_ready, 1)
            first_block(0)
            pe.wait_ge(vec_landed, len(VECTORS) * 16)
            nc.tensor.transpose(ps_a[:, 0:P], ada_row[:, 0:P], ident)
            nc.tensor.transpose(ps_a[:, P:2 * P], ada_row[:, P:2 * P], ident)
            nc.tensor.transpose(ps_a[:, 2 * P:V_ALL], ada_row[0:V_ALL - 2 * P, 2 * P:3 * P],
                                ident[0:NT, 0:NT]).then_inc(vec_psum, 1)
            ada_turn(0, first=True)
            pe.wait_ge(x_landed, 3 * 16)
            for t in range(NT):
                if t >= BANKS:
                    pe.wait_ge(x_ready, t - BANKS + 1)
                cols = slice(t * P, (t + 1) * P)
                for k in range(2):
                    nc.tensor.transpose(bank[t % BANKS][:, k * P:(k + 1) * P], x_rows[:, k, cols], ident)
                nc.tensor.transpose(bank[t % BANKS][:, PROMPT:TOK], x_rows[0:NS, 2, cols],
                                    ident[0:NS, 0:NS]).then_inc(x_psum, 1)
            first_block(1)
            ada_turn(1)
            pe.wait_ge(hist_landed, 2 * 16)
            for t in range(PT):
                g = C_HIST + NS * (t // 2)
                mm(ps_b[:, NS * t:NS * (t + 1)], hist[0:NS * HIST, t * P:(t + 1) * P],
                   cst[0:NS * HIST, g:g + NS], start=True, stop=True)
            for t in range(PT):
                c0 = PT * NS + NS * CH * t
                r = nc.tensor.transpose(ps_b[:, c0:c0 + NS * CH], hist[0:NS * CH, (PT + t) * P:(PT + t + 1) * P],
                                        ident[0:NS * CH, 0:NS * CH])
            r.then_inc(hist_psum, 1)

            def in_unit(q, i, j):
                unit(j, q * 16 + i * 4 + j, q * 64 + i * 16 + 4 * j, (U, q * 8), (U, q * 8 + KC))

            with pe.Fori(0, 3) as q:
                with pe.Fori(0, 4) as i:
                    for j in range(4):
                        ada_unit(q * 4 + i + 2, j)
                        pe.wait_ge(u_ready, q + 1)
                        in_unit(q, i, j)
                    ada_turn(q * 4 + i + 2)
            pe.wait_ge(u_ready, 4)
            with pe.Fori(0, 4) as i:
                for j in range(4):
                    ada_unit(i + A_LAST, j)
                    in_unit(3, i, j)
                ada_turn(i + A_LAST)

            pe.wait_ge(proj_ready, 1)
            for t in range(PT):
                b, cols = (ps_a, ps_b)[t // 4], slice(t % 4 * P, t % 4 * P + P)
                r = nc.tensor.transpose(b[0:HIST + NS, cols], PB[:, Z + t, PROMPT - HIST:TOK], ident)
            r.then_inc(z_psum, 1)
            for t in range(PT):
                b, cols = (ps_ada, ps_adat)[t // 4], slice(t % 4 * P, t % 4 * P + P)
                r = nc.tensor.transpose(b[0:CH + NS, cols], PB[:, CC + t, PROMPT - CH:TOK], ident)
            r.then_inc(v_psum, 1)

            pe.wait_ge(pooled_ready, 1)
            for g in range(4):
                pe.wait_ge(unit_split, split_done(U_GRP + g))
                for m in range(2):
                    t = 2 * g + m
                    pe.wait_ge(psum_free, bank_free(T_GRP + t))
                    for c in range(2):
                        k = 2 * g + c
                        r = three(bank[t % BANKS][:, 0:TOK], w_of(g % HL, c, m, 2 * P), U[:, POOL_HI + k, :],
                                  U[:, POOL_LO + k, :], c == 0, c == 1)
                    r.then_inc(part_done, MT // 2)

            def up_block(n, with_ada):
                for j in range(4):
                    if with_ada:
                        ada_unit(n + A_UP, j)
                    k = KC * (j % 2)
                    hi, lo = (((H, YP_HI + k), (H, YP_LO + k)), ((U, CONV_HI + k), (U, CONV_LO + k)))[j // 2]
                    if j < 2:
                        pe.wait_ge(yp_ready, j + 1)
                    else:
                        pe.wait_ge(yc_ready, 1)
                    unit(j, n * 4 + U_UP + j, n * 8 + T_UP + 4 * (j // 2), hi, lo, j % 2 == 0, j % 2 == 1)
                if with_ada:
                    ada_turn(n + A_UP)

            pe.wait_ge(v_staged, 2)
            with pe.Fori(0, 3) as n:
                up_block(n, True)
            up_block(3, False)

            def open_sum():
                mm(ps_a[:, TOK:TOK + 2], ones, ones[:, 0:2], start=True, stop=False)

            def add_up(l, n, end=False):
                pe.wait_ge(ln_in, n + 1 + 4 * l)
                for c in range(4):
                    r = mm(ps_a[:, 0:TOK], ones, tile_of(X, n * 4 + c), start=False, stop=end and c == 3)
                if end:
                    r.then_inc(ln_mean, 1)

            def wo_block(n, with_ada):
                for j in range(4):
                    if with_ada:
                        ada_unit(n + A_WO, j)
                    if j == 2 and not (isinstance(n, int) and n == 0):
                        add_up(0, n - 1)
                    pe.wait_ge(mixed_ready, j + 1)
                    unit(j, n * 4 + U_WO + j, n * 4 + T_WO, (H, MIX_HI + KC * j), (U, MIX_LO + KC * j), j == 0, j == 3)
                if with_ada:
                    ada_turn(n + A_WO)

            pe.wait_ge(avg_ready, 1)
            open_sum()
            wo_block(0, True)
            with pe.Fori(1, 3) as n:
                wo_block(n, True)
            wo_block(3, False)

            def norm(l):
                add_up(l, 3, end=True)
                for c in range(4):
                    pe.wait_ge(ln_sq, 4 * l + c + 1)
                    for t in range(4 * c, 4 * c + 4):
                        r = mm(ps_b[:, 0:TOK], ones, G[:, NT + t, :], start=t == 0, stop=t == NT - 1)
                r.then_inc(ln_var, 1)

            norm(0)

            def ff1_block(q, i):
                for j in range(4):
                    pe.wait_ge(u2_ready, j + 1)
                    unit(j, q * 32 + i * 4 + U_FF + j, q * 32 + i * 4 + T_FF, (U, 8 * j), (U, 8 * j + KC), j == 0, j == 3)

            def ff2_block(q, i, mean=False):
                for j in range(4):
                    if mean and j == 2:
                        add_up(1, i - 1)
                    pe.wait_ge(h_ready, q * 4 + j + 1)
                    unit(j, q * 32 + i * 4 + U_FF + 16 + j, q * 32 + i * 4 + T_FF + 16, (H, KC * j), (H, H_LO + KC * j), j == 0, j == 3)

            with pe.Fori(0, 3) as q:
                with pe.Fori(0, 4) as i:
                    ff1_block(q, i)
                with pe.Fori(0, 4) as i:
                    ff2_block(q, i)
            with pe.Fori(0, 4) as i:
                ff1_block(3, i)
            open_sum()
            ff2_block(3, 0)
            with pe.Fori(1, 4) as i:
                ff2_block(3, i, mean=True)
            norm(1)
            for c in range(4):
                pe.wait_ge(y_ready, c + 1)
                for t in range(3):
                    k = 3 * c + t
                    if k >= BANKS:
                        pe.wait_ge(y_staged, k - BANKS + 1)
                    n, at = (P, t * P) if t < 2 else (NS, PROMPT)
                    for m in range(MT):
                        r = nc.tensor.transpose(bank[k % BANKS][0:n, m * P:(m + 1) * P],
                                                X[:, MT * c + m, at:at + n], ident)
                    r.then_inc(y_psum, 1)


_INS = ["x_prompt", "x_sample", "state_pool", "state_conv", "c_prompt", "c_sample", "w_ada", "b_ada", "w_in",
        "pool_grp_w", "pool_scale", "conv_w", "w_pool_up", "w_conv_up", "w_o", "ln1_g", "ln1_b", "w_ff1", "b_ff1",
        "w_ff2", "b_ff2", "ln2_g", "ln2_b"]
_OUTS = {"y_prompt": (1, PROMPT, D), "y_sample": (NS, 1, D), "new_pool_prompt": (1, 1, HIST, D // 2),
         "new_conv_prompt": (1, 1, CH, D // 2), "new_pool_sample": (1, NS, HIST, D // 2),
         "new_conv_sample": (1, NS, CH, D // 2)}


def constants(np):
    c = np.zeros((P, C_ALL), np.float32)
    c[:, C_ID:C_ID + P] = np.eye(P, dtype=np.float32)
    for g in range(4):
        c[32 * g:32 * g + SEQS, C_SEL:C_SEL + SEQS] = np.eye(SEQS, dtype=np.float32)
    for g, w in enumerate(POOL_W):
        for t in range(16):
            c[:, C_FIX + 16 * g + t] = w / min(w, t + 1)
        for s in range(NS):
            for h in range(HIST - (w - 1), HIST):
                c[s * HIST + h, C_HIST + NS * g + s] = 1.0
    return c


def kernel(**inputs):
    import numpy as _np
    import concourse.bacc as _bacc
    from concourse.bass_utils import run_bass_kernel_spmd as _run

    nc = _bacc.Bacc("TRN2", target_bir_lowering=False, num_devices=1)
    arrays = {f"in_{n}": _np.ascontiguousarray(inputs[n]) for n in _INS}
    arrays["in_cst"] = constants(_np)
    ins = {k[3:]: nc.dram_tensor(k, v.shape, F32, kind="ExternalInput").ap() for k, v in arrays.items()}
    outs = {n: nc.dram_tensor(f"out_{n}", s, F32, kind="ExternalOutput").ap() for n, s in _OUTS.items()}
    build_layer(nc, ins, outs)
    r = _run(nc, [arrays], core_ids=[0]).results[0]
    return tuple(r[f"out_{n}"] for n in _OUTS)
```

```python
from contextlib import ExitStack

import concourse.bass as bass
from concourse import mybir

F32 = mybir.dt.float32
F32R = mybir.dt.float32r
ALU = mybir.AluOpType
ACT = mybir.ActivationFunctionType
ds = bass.ds

P = 128
D = 2048
PROMPT = 256
NS = 8
TOK = PROMPT + NS
SEQS = 1 + NS
NT = D // P
PT = NT // 2
POOL_W = (2, 4, 8, 16)
HIST = max(POOL_W) - 1
CH = 2
TAPS = 3
FF = 4 * D
EPS = 1e-5
ALPHA = 2.0 ** 0.25

KC = 4
UC = 512
MT = UC // P
US = KC * UC
RAW = 4
HL = 2
BANKS = 4
AR = 2
ADA_UNITS = D // P // KC
GW = 512

X_BANKS = BANKS + 2
X_ACT = NT - X_BANKS

U_GRP = 64
U_UP = U_GRP + 4
U_WO = U_UP + 16
U_FF = U_WO + 16
T_GRP = 4 * U_GRP
T_UP = T_GRP + PT
T_WO = T_UP + 2 * NT
T_FF = T_WO + NT
A_LAST = 14
A_UP = 18
A_WO = 21
GROUP = 3
G_LAST = 8
G_UP = 10
G_WO = 11
G_ALL = 12

V_BFF1, V_PSCALE, V_CONV, V_G1, V_B1 = 0, 64, 72, 96, 112
V_BADA, V_BFF2, V_G2 = 128, 224, 240
V_B2 = 256
V_ALL = 272
VECTORS = ((V_BFF1, 4 * NT, "b_ff1"), (V_PSCALE, PT, "pool_scale"), (V_CONV, TAPS * PT, "conv_w"),
           (V_G1, NT, "ln1_g"), (V_B1, NT, "ln1_b"), (V_BADA, 6 * NT, "b_ada"),
           (V_BFF2, NT, "b_ff2"), (V_G2, NT, "ln2_g"), (V_B2, NT, "ln2_b"))
SH1, SC1, GA1, SH2, SC2, GA2 = (NT * i for i in range(6))
C_AT = (GROUP - 1) * SEQS
C_ID, C_SEL = 0, 128
C_FIX = C_SEL + GROUP * SEQS
C_HIST = C_FIX + 64
C_ALL = C_HIST + 4 * NS

POOL_HI, POOL_LO, WIN, CONV_HI, MIX_LO = 0, 8, 16, 16, 24
Z, XC, BC, CC = 0, 8, 16, 24
MIX_HI, H_LO = 16, 16
V_AT = 32


def build_layer(nc, a, o):
    with ExitStack() as ctx:
        def sb(name, shape, dt=F32):
            return ctx.enter_context(nc.sbuf_tensor(name, shape, dt))

        def overlay(name, shape, dt, offset):
            return nc.alloc_sbuf_tensor_at(name, shape, dt, offset=offset)

        def here():
            return nc.sbuf_base + (-nc.sbuf_base) % 32

        def sem(name):
            return ctx.enter_context(nc.semaphore(name))

        raw = sb("raw", [P, RAW, US])
        w_hi = sb("w_hi", [P, HL, US], F32R)
        at_w = here()
        w_lo = sb("w_lo", [P, HL, US], F32R)
        ada_raw = sb("ada_raw", [P, AR, US])
        X = sb("X", [P, NT, TOK])
        at_u = here()
        Uf = sb("Uf", [P, 2 * NT, TOK])
        U = overlay("U", [P, 2 * NT, TOK], F32R, at_u)
        M = overlay("M", [P, NT, TOK], F32R, at_u + MIX_LO * TOK * 4)
        Mf = overlay("Mf", [P, NT, TOK], F32, at_u + MIX_LO * TOK * 4)
        at_p = here()
        assert at_p == at_u + 2 * NT * TOK * 4
        PB = sb("PB", [P, 2 * NT, TOK])
        H = overlay("H", [P, 2 * NT, TOK], F32R, at_p)
        G = sb("G", [P, 2 * NT, TOK])
        vec = sb("vec", [P, V_ALL])
        ada = sb("ada", [P, 6 * NT, SEQS])
        c_t = sb("c_t", [P, NT, C_AT + 32])
        ada_row = sb("ada_row", [P, UC])
        cst = sb("cst", [P, C_ALL])
        hist_sum = sb("hist_sum", [P, PT, NS])
        hist_conv = sb("hist_conv", [P, PT, NS * CH])
        small = sb("small", [P, MT, NS])
        ident = cst[:, C_ID:C_ID + P]
        hist = Uf[:, 24:32, :].rearrange("p t n -> p (t n)")
        x_rows = Uf[:, 8:24, :].rearrange("p t n -> p (t n)")[:, 0:2 * D].rearrange("p (k n) -> p k n", k=2)
        x_sample = overlay("x_sample", [P, D], F32, at_w + US * 4)[0:NS, :]
        first_ada = [w[:, :, :].rearrange("p t n -> p (t n)")[:, 0:ADA_UNITS * US]
                     .rearrange("p (u c n) -> p u c n", u=ADA_UNITS, c=KC) for w in (PB, G)]
        zs = PB[:, 28:32, :].rearrange("p t n -> p (t n)")
        vs = PB[:, 4:8, :].rearrange("p t n -> p (t n)")
        ones = hist_conv[:, :, :].rearrange("p t s -> p (t s)")
        rstd = ada_raw[:, 0, 0:TOK]
        mu = ada_raw[:, 1, 0:TOK]
        seq_tmp = ada_raw[:, 1, 528:528 + NT * SEQS].rearrange("p (t s) -> p t s", t=NT)
        res_bias = ada_raw[:, 1, 672:672 + NT * SEQS].rearrange("p (t s) -> p t s", t=NT)
        res_scale = ada_raw[:, 1, 816:816 + NT]
        alpha_b = ada_raw[:, 1, 832:832 + NT]
        pair, sum_x = Uf[:, 8:10, :], Uf[:, 10:12, :]
        early_sum, last_sum, early_mean, guess, off, var = (Uf[:, 16 + i, :] for i in range(6))

        bank = [ctx.enter_context(nc.psum_tensor(f"main{i}", [P, 512], F32)) for i in range(BANKS)]
        ps_ada = ctx.enter_context(nc.psum_tensor("ps_ada", [P, 512], F32))
        ps_adat = ctx.enter_context(nc.psum_tensor("ps_adat", [P, 512], F32))
        ps_a = ctx.enter_context(nc.psum_tensor("ps_a", [P, 512], F32))
        ps_b = ctx.enter_context(nc.psum_tensor("ps_b", [P, 512], F32))

        raw_landed = [sem(f"raw_landed{i}") for i in range(RAW)]
        ada_landed = [sem(f"ada_landed{i}") for i in range(AR)]
        first_landed = [sem(f"first_landed{i}") for i in range(2 * ADA_UNITS)]
        c_landed, x_landed, rest_landed, vec_landed, hist_landed = (
            sem("c_landed"), sem("x_landed"), sem("rest_landed"), sem("vec_landed"), sem("hist_landed"))
        hi_ready = sem("hi_ready")
        unit_split = sem("unit_split")
        first_rows = sem("first_rows")
        part_done = sem("part_done")
        psum_free = sem("psum_free")
        ada_used = sem("ada_used")
        row_copied = sem("row_copied")
        adat_ready = sem("adat_ready")
        ada_ready = sem("ada_ready")
        c_t_psum, c_t_ready = sem("c_t_psum"), sem("c_t_ready")
        vec_psum, vec_ready = sem("vec_psum"), sem("vec_ready")
        hist_psum, hist_ready = sem("hist_psum"), sem("hist_ready")
        x_psum, x_ready = sem("x_psum"), sem("x_ready")
        zeroed = sem("zeroed")
        u_ready = sem("u_ready")
        z_ready, proj_ready = sem("z_ready"), sem("proj_ready")
        state_psum, state_staged = sem("state_psum"), sem("state_staged")
        gates_ready, sig_ready, x_scaled = sem("gates_ready"), sem("sig_ready"), sem("x_scaled")
        pooled_ready, yp_ready, yc_ready, mixed_ready = (
            sem("pooled_ready"), sem("yp_ready"), sem("yc_ready"), sem("mixed_ready"))
        avg_ready, ln_in, ln_mean, ln_d, ln_sq, ln_sums, ln_moment, ln_var, ln_std, ln_norm = (
            sem("avg_ready"), sem("ln_in"), sem("ln_mean"), sem("ln_d"), sem("ln_sq"), sem("ln_sums"),
            sem("ln_moment"), sem("ln_var"), sem("ln_std"), sem("ln_norm"))
        mu_ready, ln_centred = sem("mu_ready"), sem("ln_centred")
        u2_coef, u2_hi_ready, u2_ready, res_ready, sum_zeroed = (
            sem("u2_coef"), sem("u2_hi_ready"), sem("u2_ready"), sem("res_ready"), sem("sum_zeroed"))
        r_ready, h_hi_ready, h_ready = sem("r_ready"), sem("h_hi_ready"), sem("h_ready")
        y_tiles, y_tail, y_psum, y_by_act, y_by_dve = (
            sem("y_tiles"), sem("y_tail"), sem("y_psum"), sem("y_by_act"), sem("y_by_dve"))
        state_out, stage_out, y_out = sem("state_out"), sem("stage_out"), sem("y_out")

        def rows(w):
            return w.rearrange("(u c p) n -> u p c n", c=KC, p=P)

        w_ada, w_in, w_pu, w_cu, w_o, w_ff1, w_ff2 = (
            rows(a[n][0]) for n in ("w_ada", "w_in", "w_pool_up", "w_conv_up", "w_o", "w_ff1", "w_ff2"))
        w_grp = a["pool_grp_w"][0].rearrange("g (c p) n -> g p c n", p=P)
        ada_u = ada_raw[:, :, :].rearrange("p s (c n) -> p s c n", c=KC)

        x_bank = bank + [ps_a, ps_b]
        y_bank = bank + [ps_ada, ps_adat, ps_a, ps_b]
        by_dve = [(0, 0), (0, 1), (1, 0), (1, 1), (2, 0), (3, 0)]
        by_act = [(0, 2), (1, 2), (2, 1), (2, 2), (3, 1), (3, 2)]

        def wait_y_copied(eng, c, t):
            if (c, t) in by_dve:
                eng.wait_ge(y_by_dve, by_dve.index((c, t)) + 1)
            else:
                eng.wait_ge(y_by_act, by_act.index((c, t)) + 1)

        def landed(n):
            return 16 * (n + 1)

        def slot_free(n):
            return n + 1

        def split_slot_free(n):
            return (n + 1) * MT

        def done(n, m=MT - 1):
            return (n + HL) * MT + m + 1

        def split_done(n):
            return RAW + n + 1

        def bank_free(t):
            return t + 1

        block = ctx.enter_context(nc.Block())

        @block.sync
        def _(sp):
            def load_main(s, n, src, size=US):
                sp.wait_ge(unit_split, slot_free(n))
                chunks = size // src.shape[-1]
                dst = raw[:, s, 0:size].rearrange("p (c n) -> p c n", c=chunks)
                sp.dma_start(dst, src).then_inc(raw_landed[s], 16)

            def load_ada(b, u, col):
                s = u % AR
                sp.wait_ge(ada_used, slot_free(ADA_UNITS * (b - 2) + u))
                sp.dma_start(ada_u[:, s], w_ada[u][:, :, ds(col, UC)]).then_inc(ada_landed[s], 16)

            def load_rows(at, rows_, name):
                c, r = divmod(at, P)
                src = a[name][0]
                src = (src.rearrange("k (r n) -> (k r) n", n=P) if len(src.shape) == 2
                       else src.rearrange("(r n) -> r n", n=P))
                sp.dma_start(ada_row[r:r + rows_, c * P:(c + 1) * P], src).then_inc(vec_landed, 16)

            sp.dma_start(raw[0:SEQS - NS, 3, :], a["c_prompt"]).then_inc(c_landed, 16)
            sp.dma_start(raw[SEQS - NS:SEQS, 3, :], a["c_sample"]).then_inc(c_landed, 16)
            sp.dma_start(cst[:, :], a["cst"]).then_inc(c_landed, 16)
            for u in range(ADA_UNITS):
                sp.dma_start(first_ada[0][:, u], w_ada[u][:, :, SH1 * P:SH1 * P + UC]).then_inc(first_landed[u], 16)
                for at, n, name in VECTORS[3 * u:3 * u + 3]:
                    load_rows(at, n, name)
            xp = a["x_prompt"][0].rearrange("(t p) n -> t p n", p=P)
            for t in range(2):
                sp.dma_start(x_rows[:, t, 0:UC], xp[t][:, 0:UC]).then_inc(x_landed, 16)
            sp.dma_start(x_sample, a["x_sample"][:, 0, :]).then_inc(x_landed, 16)
            for u in range(ADA_UNITS):
                sp.dma_start(first_ada[1][:, u], w_ada[u][:, :, SC1 * P:SC1 * P + UC]).then_inc(
                    first_landed[ADA_UNITS + u], 16)
            for t in range(2):
                sp.dma_start(x_rows[:, t, UC:D], xp[t][:, UC:D]).then_inc(rest_landed, 16)
            sp.wait_ge(c_t_psum, 1)
            with sp.Fori(0, 3) as q:
                with sp.Fori(0, 4) as i:
                    n0 = sp.snap(q * 16 + i * 4)
                    for j in range(4):
                        load_main(j, n0 + j, w_in[ds(q, 1)][0][:, :, ds((i * 4 + j) * UC, UC)])
                        load_ada(q * 4 + i + 2, j, (i * 16 + q * 4 + 4) * P)
            with sp.Fori(0, 4) as i:
                for j in range(4):
                    load_main(j, i * 4 + 48 + j, w_in[3][:, :, ds((i * 4 + j) * UC, UC)])
                    load_ada(i + A_LAST, j, (i * 4 + SC2 + 4) * P)
            for g in range(4):
                load_main(g, U_GRP + g, w_grp[g], GW)

            def load_up(n, with_ada):
                for j in range(4):
                    load_main(j, n * 4 + U_UP + j, (w_pu if j < 2 else w_cu)[j % 2][:, :, ds(n * UC, UC)])
                    if with_ada:
                        load_ada(n + A_UP, j, (n * NT + GA1) * P)

            def load_wo(n, with_ada):
                for j in range(4):
                    load_main(j, n * 4 + U_WO + j, w_o[j][:, :, ds(n * UC, UC)])
                    if with_ada:
                        load_ada(n + A_WO, j, (n * 4 + GA2 + 4) * P)

            with sp.Fori(0, 3) as n:
                load_up(n, True)
            load_up(3, False)
            with sp.Fori(0, 3) as n:
                load_wo(n, True)
            load_wo(3, False)
            with sp.Fori(0, 4) as q:
                with sp.Fori(0, 4) as i:
                    for j in range(4):
                        load_main(j, q * 32 + i * 4 + U_FF + j, w_ff1[j][:, :, ds((q * 4 + i) * UC, UC)])
                with sp.Fori(0, 4) as i:
                    for j in range(4):
                        load_main(j, q * 32 + i * 4 + U_FF + 16 + j,
                                  w_ff2[ds(q * 4 + j, 1)][0][:, :, ds(i * UC, UC)])
            yp = o["y_prompt"][0].rearrange("(t p) n -> t p n", p=P)
            for c, t in ((0, 0), (0, 1), (1, 0), (1, 1), (0, 2), (1, 2), (2, 0), (2, 1), (2, 2), (3, 0), (3, 1), (3, 2)):
                cols = slice(c * UC, (c + 1) * UC)
                wait_y_copied(sp, c, t)
                if t < 2:
                    sp.dma_start(yp[t][:, cols], raw[:, t, cols]).then_inc(y_out, 16)
                else:
                    sp.dma_start(o["y_sample"][:, 0, cols], raw[0:NS, t, cols]).then_inc(y_out, 16)
            sp.wait_ge(y_out, 12 * 16)

        @block.gpsimd
        def _(pool):
            nc.gpsimd.memset(c_t[:, :, :], 0.0).then_inc(zeroed, 1)
            pool.dma_start(hist[0:NS * HIST, 0:PT * P],
                           a["state_pool"][0].rearrange("s h n -> (s h) n")).then_inc(hist_landed, 16)
            pool.dma_start(hist[0:NS * CH, PT * P:2 * PT * P],
                           a["state_conv"][0].rearrange("s h n -> (s h) n")).then_inc(hist_landed, 16)
            pool.dma_start(o["new_pool_sample"][0][:, 0:HIST - 1, :],
                           a["state_pool"][0][:, 1:HIST, :]).then_inc(state_out, 16)
            pool.dma_start(o["new_conv_sample"][0][:, 0:CH - 1, :],
                           a["state_conv"][0][:, 1:CH, :]).then_inc(state_out, 16)

            g_tt, g_ts, g_cp = nc.gpsimd.tensor_tensor, nc.gpsimd.tensor_scalar, nc.gpsimd.tensor_copy
            z8 = PB[:, Z:Z + PT, :]
            A8, B8 = Uf[:, POOL_LO:POOL_LO + PT, :], Uf[:, WIN:WIN + PT, :]
            pool.wait_ge(hist_ready, 1)
            pool.wait_ge(z_ready, 1)

            def window(dst, src, first, step):
                g_tt(dst[:, first:PT, step:PROMPT], src[:, first:PT, step:PROMPT],
                     src[:, first:PT, 0:PROMPT - step], ALU.add)
                g_cp(dst[:, first:PT, 0:step], src[:, first:PT, 0:step])
                pool.drain()

            window(A8, z8, 0, 1)
            window(B8, A8, 2, 2)
            window(A8, B8, 4, 4)
            window(B8, A8, 6, 8)
            sums = [A8[:, 0:2], B8[:, 2:4], A8[:, 4:6], B8[:, 6:8]]
            for g, s in enumerate(sums):
                two = slice(2 * g, 2 * g + 2)
                fix = cst[:, C_FIX + 16 * g:C_FIX + 16 * g + 16].unsqueeze(1).to_broadcast([P, 2, 16])
                g_tt(s[:, :, 0:16], s[:, :, 0:16], fix, ALU.mult)
                g_tt(s[:, :, PROMPT:TOK], PB[:, two, PROMPT:TOK], hist_sum[:, two, :], ALU.add)
            pool.drain()
            for g, s in enumerate(sums):
                g_ts(A8[:, 2 * g:2 * g + 2, :], s, 1.0 / POOL_W[g], None, ALU.mult)
            pool.drain()
            g_tt(A8, A8, z8, ALU.subtract)
            pool.drain()
            g_cp(U[:, POOL_HI:POOL_HI + PT, :], A8)
            pool.drain()
            g_tt(U[:, POOL_LO:POOL_LO + PT, :], A8, U[:, POOL_HI:POOL_HI + PT, :].bitcast(F32),
                 ALU.subtract).then_inc(pooled_ready, 1)

            pool.wait_ge(state_staged, 4)
            for dst, src in ((o["new_pool_prompt"][0][0], zs[0:HIST]),
                             (o["new_pool_sample"][0][:, HIST - 1, :], zs[HIST:HIST + NS]),
                             (o["new_conv_prompt"][0][0], vs[V_AT:V_AT + CH]),
                             (o["new_conv_sample"][0][:, CH - 1, :], vs[V_AT + CH:V_AT + CH + NS])):
                pool.dma_start(dst, src[:, 0:PT * P]).then_inc(stage_out, 16)
            pool.wait_ge(state_out, 2 * 16)
            pool.wait_ge(stage_out, 4 * 16)

            pool.wait_ge(part_done, done(U_WO - 1))
            nc.gpsimd.memset(sum_x, 0.0).then_inc(sum_zeroed, 1)

            def per_seq(col):
                return vec[:, col:col + NT].unsqueeze(2).to_broadcast([P, NT, SEQS])

            sc2, sh2, ga2 = ada[:, SC2:SC2 + NT, :], ada[:, SH2:SH2 + NT, :], ada[:, GA2:GA2 + NT, :]
            pool.wait_ge(ada_ready, G_ALL)
            g_tt(seq_tmp, sc2, per_seq(V_B1), ALU.mult)
            pool.drain()
            g_tt(sh2, sh2, seq_tmp, ALU.add)
            g_tt(sc2, sc2, per_seq(V_G1), ALU.mult)
            pool.drain().then_inc(u2_coef, 1)

            g_ts(res_scale, vec[:, V_G1:V_G1 + NT], ALPHA, None, ALU.mult)
            g_ts(alpha_b, vec[:, V_B1:V_B1 + NT], ALPHA, None, ALU.mult)
            g_tt(res_bias, ga2, per_seq(V_BFF2), ALU.mult)
            pool.drain()
            g_tt(res_bias, res_bias, alpha_b.unsqueeze(2).to_broadcast([P, NT, SEQS]), ALU.add)
            pool.drain()

            def minus_mean(l):
                pool.wait_ge(mu_ready, l + 1)
                pool.wait_ge(ln_sq, 4 * l + 4)
                for c in range(1, 4):
                    t4 = slice(4 * c, 4 * c + 4)
                    g_tt(G[:, t4, :], X[:, t4, :], mu.unsqueeze(1).to_broadcast([P, 4, TOK]),
                         ALU.subtract).then_inc(ln_centred, 1)

            minus_mean(0)
            pool.wait_ge(ln_norm, 4)
            for t in range(NT):
                g_ts(X[:, t, 0:PROMPT], G[:, t, 0:PROMPT], res_scale[:, t:t + 1], res_bias[:, t, 0:1],
                     ALU.mult, ALU.add)
            xs = X[:, :, PROMPT:TOK]
            g_tt(xs, G[:, 0:NT, PROMPT:TOK], res_scale.unsqueeze(2).to_broadcast([P, NT, NS]), ALU.mult)
            pool.drain()
            g_tt(xs, xs, res_bias[:, :, 1:SEQS], ALU.add)
            pool.drain().then_inc(res_ready, 1)

            pool.wait_ge(part_done, done(U_FF + 3 * 32 + 15))
            nc.gpsimd.memset(sum_x, 0.0).then_inc(sum_zeroed, 1)
            minus_mean(1)
            pool.wait_ge(ln_norm, 8)
            for t in range(12, 16):
                last = g_ts(X[:, t, :], G[:, t, :], vec[:, V_G2 + t:V_G2 + t + 1], vec[:, V_B2 + t:V_B2 + t + 1],
                            ALU.mult, ALU.add)
            last.then_inc(y_tail, 1)

        @block.scalar
        def _(act):
            def hi_part(s, nth, n, size=US):
                act.wait_ge(raw_landed[s], landed(nth))
                act.wait_ge(part_done, split_slot_free(n))
                nc.scalar.activation(w_hi[:, s % HL, 0:size], raw[:, s, 0:size], ACT.Copy).then_inc(hi_ready, 1)

            def copy_row(g, b):
                if isinstance(b, int) and b < 2:
                    act.wait_ge(first_rows, b + 1)
                else:
                    act.wait_ge(ada_used, (b - 1) * ADA_UNITS + AR)
                if isinstance(b, int) and b == 0:
                    act.wait_ge(vec_psum, 1)
                else:
                    act.wait_ge(adat_ready, g)
                nc.scalar.copy(ada_row[:, :], ps_ada[:, :]).then_inc(row_copied, 1)

            def copy_x(tiles):
                for t in tiles:
                    act.wait_ge(x_psum, t + 1)
                    nc.scalar.copy(X[:, t, :], x_bank[t % len(x_bank)][:, 0:TOK]).then_inc(x_ready, 1)

            copy_row(0, 0)
            copy_x(range(KC))
            copy_row(1, 1)
            copy_x(range(KC, X_ACT))
            hi_part(0, 0, 0)
            with act.Fori(0, 3) as q:
                with act.Fori(0, 2) as h:
                    for e in range(2):
                        b = act.snap(q * 4 + h * 2 + e)
                        n0 = act.snap(q * 16 + h * 8 + 4 * e)
                        for j in range(4):
                            if j == 3 and e == 1:
                                copy_row(q * 2 + h + 2, b + 2)
                            hi_part((j + 1) % RAW, b + (j + 1) // 4, n0 + (j + 1))
            act.wait_ge(u_ready, 4)
            nc.scalar.mul(X[:, :, :], X[:, :, :], ALPHA).then_inc(x_scaled, 1)
            for i in range(3):
                for j in range(4):
                    if j == 3 and i == 1:
                        copy_row(G_LAST, A_LAST + 1)
                    hi_part((j + 1) % RAW, i + 12 + (j + 1) // 4, i * 4 + 48 + (j + 1))

            def sigmoid(t, n, count):
                act.wait_ge(gates_ready, count)
                return nc.scalar.activation(G[:, t:t + n, :], G[:, t:t + n, :], ACT.Sigmoid)

            for j in range(4):
                if j == 3:
                    copy_row(G_LAST + 1, A_LAST + 3)
                hi_part((j + 1) % RAW, 15 + (j + 1) // 4, 60 + j + 1, US if j < 3 else GW)
                sigmoid(*((0, 8, 1), (8, 8, 1), (16, 4, 2), (20, 8, 4))[j])
            hi_part(1, 16, U_GRP + 1, GW)
            sigmoid(28, 4, 5).then_inc(sig_ready, 1)
            for j in range(1, 4):
                hi_part((j + 1) % RAW, 16 + (j + 1) // 4, U_GRP + j + 1, GW if j < 3 else US)
            act.wait_ge(state_psum, 1)
            for rows_, stage in ((slice(0, HIST + NS), zs), (slice(V_AT, V_AT + CH + NS), vs)):
                nc.scalar.copy(stage[rows_, 0:512], ps_a[rows_, :]).then_inc(state_staged, 1)
                nc.scalar.copy(stage[rows_, 512:1024], ps_b[rows_, :]).then_inc(state_staged, 1)

            def hi_up(n, turn=False):
                for j in range(4):
                    if j == 3 and turn:
                        copy_row(G_UP, A_UP + 2)
                    hi_part((j + 1) % RAW, n + 17 + (j + 1) // 4, n * 4 + U_UP + j + 1)

            def hi_wo(n, turn=False):
                for j in range(4):
                    if j == 3 and turn:
                        copy_row(G_WO, A_WO + 2)
                    hi_part((j + 1) % RAW, n + 21 + (j + 1) // 4, n * 4 + U_WO + j + 1)

            with act.Fori(0, 2) as n:
                hi_up(n)
            hi_up(2, turn=True)
            hi_up(3)
            with act.Fori(0, 2) as n:
                hi_wo(n)
            hi_wo(2, turn=True)

            def squares(l, c):
                act.wait_ge(ln_d, 4 * l + c + 1)
                nc.scalar.activation(G[:, NT + 4 * c:NT + 4 * c + 4, :], G[:, 4 * c:4 * c + 4, :],
                                     ACT.Square).then_inc(ln_sq, 1)

            def squares_at(l, j):
                if j == 1:
                    squares(l, 0)
                    squares(l, 1)
                if j == 2:
                    squares(l, 2)

            def std(l):
                nc.scalar.activation(rstd[:, 0:1], ones[:, 0:1], ACT.Sqrt)
                act.drain()
                act.wait_ge(ln_var, l + 1)
                nc.scalar.activation(rstd, var, ACT.Sqrt).then_inc(ln_std, 1)

            for j in range(4):
                hi_part((j + 1) % RAW, 24 + (j + 1) // 4, 12 + U_WO + j + 1)
                squares_at(0, j)
            squares(0, 3)
            std(0)
            hi_part(1, 25, U_FF + 1)
            for c in range(4):
                n = 2 if c == 0 else 4
                if c == 3:
                    hi_part(2, 25, U_FF + 2)
                act.wait_ge(ln_norm, c + 1)
                for t in range(4 * c, 4 * c + n):
                    nc.scalar.activation(Uf[:, t + 4 * c + 4, 0:PROMPT], G[:, t, 0:PROMPT], ACT.Identity,
                                         bias=ada[:, SH2 + t, 0:1], scale=ada[:, SC2 + t, 0:1])
                act.drain()
                nc.scalar.copy(U[:, 8 * c:8 * c + n, :], Uf[:, 8 * c + 4:8 * c + 4 + n, :]).then_inc(u2_hi_ready, 1)

            def square(b, i):
                act.wait_ge(r_ready, b)
                r = PB[:, H_LO + 4 * i:H_LO + 4 * i + 4, :]
                nc.scalar.activation(r, r, ACT.Square)
                act.drain()
                nc.scalar.copy(H[:, 4 * i:4 * i + 4, :], r).then_inc(h_hi_ready, 1)

            def ff_quarter(q, last=False):
                for i in range(4):
                    for j in range(4):
                        if j == 3:
                            square(q * 4 + i + 1, i)
                        hi_part((j + 3) % RAW, q * 8 + 25 + i + (j + 3) // 4, q * 32 + U_FF + 4 * i + j + 3)
                for i in range(4):
                    for j in range(4):
                        if not last or i < 3 or j == 0:
                            hi_part((j + 3) % RAW, q * 8 + 29 + i + (j + 3) // 4, q * 32 + U_FF + 19 + 4 * i + j)
                        if last and i == 2 and j == 3:
                            squares_at(1, 1)
                        if last and i == 3 and j == 0:
                            squares_at(1, 2)

            with act.Fori(0, 3) as q:
                ff_quarter(q)
            ff_quarter(3, last=True)
            squares(1, 3)
            std(1)
            for c in range(3):
                act.wait_ge(ln_norm, 4 + c + 1)
                for t in range(4 * c, 4 * c + 4):
                    last = nc.scalar.activation(X[:, t, :], G[:, t, :], ACT.Identity,
                                                bias=vec[:, V_B2 + t:V_B2 + t + 1], scale=vec[:, V_G2 + t:V_G2 + t + 1])
                last.then_inc(y_tiles, 1)
            for c, t in by_act:
                k = 3 * c + t
                act.wait_ge(y_psum, k + 1)
                n = P if t < 2 else NS
                nc.scalar.copy(raw[0:n, t, c * UC:(c + 1) * UC], y_bank[k % len(y_bank)][0:n, :]).then_inc(y_by_act, 1)

        @block.vector
        def _(dve):
            tt, ts, stt, cp = (nc.vector.tensor_tensor, nc.vector.tensor_scalar,
                               nc.vector.scalar_tensor_tensor, nc.vector.tensor_copy)

            def lo_part(s, n, size=US):
                dve.wait_ge(hi_ready, n + 1)
                tt(w_lo[:, s % HL, 0:size], raw[:, s, 0:size], w_hi[:, s % HL, 0:size].bitcast(F32),
                   ALU.subtract).then_inc(unit_split, 1)

            def take_ada(g, *tiles):
                dve.wait_ge(adat_ready, g + 1)
                w = len(tiles) * SEQS
                src = ps_adat[:, 0:MT * w].rearrange("p (t s) -> p t s", t=MT)
                for k, tile in enumerate(tiles):
                    at = w - SEQS * (k + 1)
                    bias = vec[:, ds(tile + V_BADA, MT)].unsqueeze(2).to_broadcast([P, MT, SEQS])
                    r = tt(ada[:, ds(tile, MT), :], src[:, :, at:at + SEQS], bias, ALU.add)
                r.then_inc(ada_ready, 1)

            def split(hi, lo, value):
                dve.drain()
                cp(hi, value)
                dve.drain()
                return tt(lo, value, hi.bitcast(F32), ALU.subtract)

            def make_u(q):
                dve.drain()
                for k in range(KC):
                    t = q * KC + k
                    ts(Uf[:, ds(q * 8 + KC + k, 1), 0:PROMPT], X[:, ds(t, 1), 0:PROMPT],
                       ada[:, ds(t + SC1, 1), 0:1].rearrange("p a b -> p (a b)"),
                       ada[:, ds(t + SH1, 1), 0:1].rearrange("p a b -> p (a b)"), ALU.mult, ALU.add)
                t = q * KC
                lo4 = ds(q * 8 + KC, KC)
                s = Uf[:, lo4, PROMPT:TOK]
                tt(s, X[:, ds(t, KC), PROMPT:TOK], ada[:, ds(t + SC1, KC), 1:SEQS], ALU.mult)
                dve.drain()
                tt(s, s, ada[:, ds(t + SH1, KC), 1:SEQS], ALU.add)

            def split_u(q):
                hi4, lo4 = ds(q * 8, KC), ds(q * 8 + KC, KC)
                split(U[:, hi4, :], U[:, lo4, :], Uf[:, lo4, :]).then_inc(u_ready, 1)

            dve.sem_inc(unit_split, RAW)
            dve.sem_inc(psum_free, BANKS)
            dve.wait_ge(zeroed, 1)
            dve.wait_ge(c_t_psum, 1)
            cp(c_t[:, :, C_AT:C_AT + SEQS], ps_adat[:, 0:NT * SEQS].rearrange("p (t s) -> p t s", t=NT)).then_inc(c_t_ready, 1)
            dve.wait_ge(vec_psum, 1)
            cp(vec[:, :], ps_a[:, 0:V_ALL]).then_inc(vec_ready, 1)
            dve.drain()
            for t in (SC1, SC2):
                v = vec[:, V_BADA + t:V_BADA + t + NT]
                ts(v, v, 1.0, None, ALU.add)
            dve.drain()
            take_ada(0, SH1)
            dve.wait_ge(hist_psum, 1)
            cp(hist_sum[:, :, :], ps_b[:, 0:PT * NS].rearrange("p (t s) -> p t s", t=PT))
            hc = ps_b[:, PT * NS:PT * NS * 3].rearrange("p (t s k) -> p t s k", t=PT, k=CH)
            hd = hist_conv[:, :, :].rearrange("p t (k s) -> p t k s", k=CH)
            for k in range(CH):
                w = vec[:, V_CONV + PT * k:V_CONV + PT * (k + 1)].unsqueeze(2).to_broadcast([P, PT, NS])
                tt(hd[:, :, k], hc[:, :, :, k], w, ALU.mult)
            dve.drain()
            tt(hd[:, :, 0], hd[:, :, 0], hd[:, :, 1], ALU.add).then_inc(hist_ready, 1)
            dve.wait_ge(x_ready, KC)
            take_ada(1, SC1)
            make_u(0)
            split_u(0)
            for t in range(X_ACT, NT):
                dve.wait_ge(x_psum, t + 1)
                cp(X[:, t, :], x_bank[t % len(x_bank)][:, 0:TOK])
            lo_part(0, 0)
            dve.wait_ge(x_ready, X_ACT)

            def conv_step(at):
                v, y = PB[:, CC:CC + PT, :], PB[:, XC:XC + PT, :]
                if at == 3:
                    dve.drain().then_inc(z_ready, 1)
                if at == 8:
                    dve.drain()
                    tt(v, v, y, ALU.mult)
                    dve.drain()
                if at == 9:
                    for t in range(PT):
                        w = V_CONV + 2 * PT + t
                        ts(y[:, t, :], v[:, t, :], vec[:, w:w + 1], None, ALU.mult)
                    dve.drain()
                if at in (10, 11):
                    k = 11 - at
                    back = TAPS - 1 - k
                    for t in range(PT):
                        w = V_CONV + PT * k + t
                        stt(y[:, t, back:PROMPT], v[:, t, 0:PROMPT - back], vec[:, w:w + 1],
                            y[:, t, back:PROMPT], ALU.mult, ALU.add)
                    dve.drain()
                if at == 12:
                    tt(y[:, :, PROMPT:TOK], y[:, :, PROMPT:TOK], hd[:, :, 0], ALU.add)
                    dve.drain()
                    tt(y, y, PB[:, BC:BC + PT, :], ALU.mult)
                if at == 13:
                    dve.drain().then_inc(proj_ready, 1)
                    dve.wait_ge(pooled_ready, 1)
                    cp(U[:, CONV_HI:CONV_HI + PT, :], y)
                if at == 14:
                    dve.drain()
                    tt(H[:, XC:XC + PT, :], y, U[:, CONV_HI:CONV_HI + PT, :].bitcast(F32),
                       ALU.subtract).then_inc(yc_ready, 1)

            def in_block(q, i, steady=True, first=False):
                for j in range(4):
                    last = not steady and i == 3 and j == 3
                    lo_part((j + 1) % RAW, q * 16 + 4 * i + j + 1, GW if last else US)
                    for m in range(MT):
                        t = 16 * i + 4 * j + m
                        dst = PB[:, t, :] if t < 32 else G[:, t - 32, :]
                        dve.wait_ge(part_done, done(q * 16 + 4 * i + j, m))
                        if first:
                            cp(dst, bank[m][:, 0:TOK]).then_inc(psum_free, 1)
                        else:
                            tt(dst, bank[m][:, 0:TOK], dst, ALU.add).then_inc(psum_free, 1)
                    if steady and i == 2 and j == 1:
                        make_u(q + 1)
                    if steady and i == 2 and j == 2:
                        split_u(q + 1)
                    if not steady:
                        if 4 * i + j >= 11:
                            dve.drain().then_inc(gates_ready, 1)
                        conv_step(4 * i + j)

            for i in range(4):
                in_block(0, i, first=True)
                if i % 2:
                    take_ada(2 + i // 2, 16 * i - 12, 16 * i + 4)
            with dve.Fori(1, 3) as q:
                for i in range(4):
                    in_block(q, i)
                    if i % 2:
                        take_ada(q * 2 + 2 + i // 2, q * 4 + 16 * i - 12, q * 4 + 16 * i + 4)
            for i in range(4):
                in_block(3, i, steady=False)
                if i == 3:
                    lo_part(1, U_GRP + 1, GW)
                if i % 2:
                    take_ada(G_LAST + i // 2, SC2 + 4 * i, SC2 + 4 + 4 * i)

            for g in range(4):
                dve.wait_ge(part_done, done(U_GRP + g))
                for m in range(2):
                    t = 2 * g + m
                    ts(Uf[:, POOL_LO + t, :], bank[t % BANKS][:, 0:TOK], vec[:, V_PSCALE + t:V_PSCALE + t + 1],
                       None, ALU.mult).then_inc(psum_free, 1)
                if g < 3:
                    lo_part((g + 2) % RAW, U_GRP + g + 2, GW if g < 2 else US)
                if g % 2:
                    hi4 = slice(POOL_HI + 2 * g - 2, POOL_HI + 2 * g + 2)
                    lo4 = slice(POOL_LO + 2 * g - 2, POOL_LO + 2 * g + 2)
                    split(U[:, hi4, :], U[:, lo4, :], Uf[:, lo4, :]).then_inc(yp_ready, 1)

            nc.vector.memset(ones, 1.0 / D).then_inc(avg_ready, 1)

            dve.wait_ge(sig_ready, 1)

            def up_block(n):
                for j in range(4):
                    lo_part((j + 1) % RAW, n * 4 + U_UP + j + 1)
                    if j % 2 == 0:
                        continue
                    for m in range(MT):
                        dve.wait_ge(part_done, done(n * 4 + U_UP + j, m))
                        g = G[:, ds(n * 4 + NT * (j // 2) + m, 1), :].rearrange("p a n -> p (a n)")
                        tt(g, bank[m][:, 0:TOK], g, ALU.mult).then_inc(psum_free, 1)
                dve.drain()
                lo = Mf[:, ds(n * 4, MT), :]
                tt(lo, G[:, ds(n * 4, MT), :], G[:, ds(n * 4 + NT, MT), :], ALU.add)
                split(H[:, ds(n * 4 + MIX_HI, MT), :], M[:, ds(n * 4, MT), :], lo).then_inc(mixed_ready, 1)

            with dve.Fori(0, 3) as n:
                up_block(n)
            take_ada(G_UP, GA1, SH2, SC2)
            dve.wait_ge(stage_out, 4 * 16)
            up_block(3)

            def add_gated(n, x0, gate):
                dve.drain()
                for m in range(MT):
                    dve.wait_ge(part_done, done(n, m))
                    xt = X[:, ds(x0 + m, 1), 0:PROMPT].rearrange("p a n -> p (a n)")
                    gt = ada[:, ds(x0 + gate + m, 1), :].rearrange("p a n -> p (a n)")
                    stt(xt, bank[m][:, 0:PROMPT], gt[:, 0:1], xt, ALU.mult, ALU.add)
                    tt(small[:, m, :], bank[m][:, PROMPT:TOK], gt[:, 1:SEQS], ALU.mult).then_inc(psum_free, 1)
                dve.drain()
                xs = X[:, ds(x0, MT), PROMPT:TOK]
                tt(xs, xs, small[:, :, :], ALU.add)

            dve.wait_ge(x_scaled, 1)

            def pairs(x0):
                dve.drain()
                tt(pair, X[:, ds(x0, 2), :], X[:, ds(x0 + 2, 2), :], ALU.add)
                dve.drain()

            def sum_in(l, x0):
                pairs(x0)
                dve.wait_ge(sum_zeroed, l + 1)
                tt(sum_x, sum_x, pair, ALU.add)

            def early_total():
                dve.drain()
                tt(early_sum, sum_x[:, 0, :], sum_x[:, 1, :], ALU.add).then_inc(ln_in, 1)

            def minus_guess(c):
                tt(G[:, 4 * c:4 * c + 4, :], X[:, 4 * c:4 * c + 4, :],
                   guess.unsqueeze(1).to_broadcast([P, 4, TOK]), ALU.subtract).then_inc(ln_d, 1)

            def early_norm(l, j):
                if j == 0:
                    dve.wait_ge(ln_mean, 2 * l + 1)
                    cp(early_mean, ps_a[:, 0:TOK])
                    ts(guess, ps_a[:, 0:TOK], NT / (NT - MT), None, ALU.mult)
                    dve.drain()
                    minus_guess(0)
                    minus_guess(1)
                if j == 1:
                    minus_guess(2)
                    dve.wait_ge(ln_sq, 4 * l + 2)
                    tt(G[:, NT:NT + 4, :], G[:, NT:NT + 4, :], G[:, NT + 4:NT + 8, :], ALU.add)
                if j == 2:
                    dve.wait_ge(ln_sq, 4 * l + 3)
                    dve.drain()
                    tt(G[:, NT:NT + 4, :], G[:, NT:NT + 4, :], G[:, NT + 8:NT + 12, :], ALU.add)
                    dve.drain()
                    tt(G[:, NT:NT + 2, :], G[:, NT:NT + 2, :], G[:, NT + 2:NT + 4, :], ALU.add)
                    dve.drain()
                    tt(G[:, NT, :], G[:, NT, :], G[:, NT + 1, :], ALU.add).then_inc(ln_sums, 1)

            def norm(l):
                dve.drain()
                minus_guess(3)
                pairs(NT - MT)
                tt(last_sum, pair[:, 0, :], pair[:, 1, :], ALU.add).then_inc(ln_in, 1)
                dve.wait_ge(ln_sq, 4 * l + 4)
                sq = G[:, 2 * NT - 4:2 * NT, :]
                tt(sq[:, 0:2], sq[:, 0:2], sq[:, 2:4], ALU.add)
                dve.drain()
                tt(G[:, NT + 1, :], sq[:, 0], sq[:, 1], ALU.add).then_inc(ln_sums, 1)
                dve.wait_ge(ln_mean, 2 * l + 2)
                tt(mu, early_mean, ps_ada[:, 0:TOK], ALU.add)
                dve.drain()
                tt(off, mu, guess, ALU.subtract).then_inc(mu_ready, 1)
                dve.drain()
                tt(off, off, off, ALU.mult)
                dve.drain()

                dve.wait_ge(ln_moment, l + 1)
                stt(var, ps_b[:, 0:TOK], EPS, off, ALU.add, ALU.subtract).then_inc(ln_var, 1)
                tt(G[:, 0:4, :], X[:, 0:4, :], mu.unsqueeze(1).to_broadcast([P, 4, TOK]), ALU.subtract)
                dve.wait_ge(ln_std, l + 1)
                nc.vector.reciprocal(rstd, rstd)
                dve.drain()

            def normalise(l, c):
                t4 = slice(4 * c, 4 * c + 4)
                if c:
                    dve.wait_ge(ln_centred, 3 * l + c)
                return tt(G[:, t4, :], G[:, t4, :], rstd.unsqueeze(1).to_broadcast([P, 4, TOK]), ALU.mult)

            with dve.Fori(0, 3) as n:
                for j in range(4):
                    lo_part((j + 1) % RAW, n * 4 + U_WO + j + 1)
                add_gated(n * 4 + U_WO + 3, n * 4, GA1)
                sum_in(0, n * 4)
            take_ada(G_WO, GA2 + 4, GA2 + 8, GA2 + 12)
            early_total()
            for j in range(4):
                lo_part((j + 1) % RAW, 12 + U_WO + j + 1)
                early_norm(0, j)
            add_gated(15 + U_WO, 12, GA1)

            def start_u2(c):
                normalise(0, c)
                dve.drain()
                s = Uf[:, 8 * c + 4:8 * c + 8, PROMPT:TOK]
                tt(s, G[:, 4 * c:4 * c + 4, PROMPT:TOK], ada[:, SC2 + 4 * c:SC2 + 4 * c + 4, 1:SEQS], ALU.mult)
                dve.drain()
                tt(s, s, ada[:, SH2 + 4 * c:SH2 + 4 * c + 4, 1:SEQS], ALU.add).then_inc(ln_norm, 1)

            def lo_u2(c, n=4):
                dve.wait_ge(u2_hi_ready, c + 1)
                tt(U[:, 8 * c + 4:8 * c + 4 + n, :], Uf[:, 8 * c + 4:8 * c + 4 + n, :],
                   U[:, 8 * c:8 * c + n, :].bitcast(F32), ALU.subtract).then_inc(u2_ready, 1)

            norm(0)
            dve.wait_ge(u2_coef, 1)
            start_u2(0)
            for t in (2, 3):
                ts(Uf[:, KC + t, 0:PROMPT], G[:, t, 0:PROMPT], ada[:, SC2 + t, 0:1], ada[:, SH2 + t, 0:1],
                   ALU.mult, ALU.add)
            split(U[:, 2:4, :], U[:, KC + 2:KC + 4, :], Uf[:, KC + 2:KC + 4, :])
            lo_u2(0, 2)
            start_u2(1)
            lo_part(1, U_FF + 1)
            start_u2(2)
            lo_u2(1)
            start_u2(3)
            lo_u2(2)
            lo_part(2, U_FF + 2)
            lo_u2(3)

            def lo_h(b, i):
                dve.wait_ge(h_hi_ready, b)
                tt(H[:, H_LO + 4 * i:H_LO + 4 * i + 4, :], PB[:, H_LO + 4 * i:H_LO + 4 * i + 4, :],
                   H[:, 4 * i:4 * i + 4, :].bitcast(F32), ALU.subtract).then_inc(h_ready, 1)

            def ff_quarter(q, last=False):
                for i in range(4):
                    for j in range(4):
                        if j == 2:
                            for m in range(MT):
                                t = 4 * i + m
                                dve.wait_ge(part_done, done(q * 32 + U_FF + 4 * i + 3, m))
                                bias = vec[:, ds(q * 16 + V_BFF1 + t, 1)]
                                r = ts(PB[:, H_LO + t, :], bank[m][:, 0:TOK], bias, 0.0, ALU.add, ALU.max)
                                r.then_inc(psum_free, 1)
                            dve.drain().then_inc(r_ready, 1)
                        if j == 3:
                            lo_h(q * 4 + i + 1, i)
                        lo_part((j + 3) % RAW, q * 32 + U_FF + 4 * i + j + 3)
                dve.wait_ge(res_ready, 1)
                for i in range(4):
                    for j in range(4):
                        if j == 2:
                            add_gated(q * 32 + U_FF + 19 + 4 * i, 4 * i, GA2)
                            if last and i < 3:
                                sum_in(1, 4 * i)
                            if last and i == 2:
                                early_total()
                        if not last or i < 3 or j == 0:
                            lo_part((j + 3) % RAW, q * 32 + U_FF + 19 + 4 * i + j)
                        if last:
                            if i == 2 and j >= 2:
                                early_norm(1, j - 2)
                            if i == 3 and j == 0:
                                early_norm(1, 2)

            with dve.Fori(0, 3) as q:
                ff_quarter(q)
            ff_quarter(3, last=True)

            norm(1)
            for c in range(4):
                normalise(1, c).then_inc(ln_norm, 1)
            for c, t in by_dve:
                k = 3 * c + t
                dve.wait_ge(y_psum, k + 1)
                cp(raw[:, t, c * UC:(c + 1) * UC], y_bank[k % len(y_bank)][:, :]).then_inc(y_by_dve, 1)

        @block.tensor
        def _(pe):
            mm = nc.tensor.matmul

            def three(out, w, x_hi, x_lo, start, stop):
                wh, wl = w
                mm(out, wh, x_hi, start=start, stop=False)
                mm(out, wh, x_lo, start=False, stop=False)
                return mm(out, wl, x_hi, start=False, stop=stop)

            def w_of(s, c, m, width=UC):
                cols = slice(c * width + m * P, c * width + (m + 1) * P)
                return w_hi[:, s, cols], w_lo[:, s, cols]

            def tile_of(tensor, t):
                return tensor[:, ds(t, 1), :].rearrange("p a n -> p (a n)")

            def unit(j, n, t0, hi, lo, first=True, last=True, early=None):
                pe.wait_ge(unit_split, split_done(n))
                for m in range(MT):
                    if early and m == MT - 1:
                        early()
                    if first:
                        pe.wait_ge(psum_free, bank_free(t0 + m))
                    for c in range(KC):
                        r = three(bank[m][:, 0:TOK], w_of(j % HL, c, m), tile_of(hi[0], hi[1] + c),
                                  tile_of(lo[0], lo[1] + c), first and c == 0, last and c == KC - 1)
                    r.then_inc(part_done, 1)

            def four_chunks(u, w, at=C_AT, first=True, last=True):
                for j in range(KC):
                    r = mm(ps_ada[32 * j:32 * j + 32, :], c_t[:, KC * u + j, ds(at, 32)], w[:, j, :],
                           start=first and u == 0, stop=last and u == ADA_UNITS - 1)
                return r

            def hist_sums():
                pe.wait_ge(hist_landed, 2 * 16)
                for t in range(PT):
                    g = C_HIST + NS * (t // 2)
                    mm(ps_b[:, NS * t:NS * (t + 1)], hist[0:NS * HIST, t * P:(t + 1) * P],
                       cst[0:NS * HIST, g:g + NS], start=True, stop=True)

            def hist_turn():
                for t in range(PT):
                    c0 = PT * NS + NS * CH * t
                    r = nc.tensor.transpose(ps_b[:, c0:c0 + NS * CH], hist[0:NS * CH, (PT + t) * P:(PT + t + 1) * P],
                                            ident[0:NS * CH, 0:NS * CH])
                r.then_inc(hist_psum, 1)

            def first_block(b, between={}):
                if b:
                    pe.wait_ge(row_copied, b)
                for u in range(ADA_UNITS):
                    pe.wait_ge(first_landed[ADA_UNITS * b + u], 16)
                    r = four_chunks(u, first_ada[b][:, u])
                    if u == ADA_UNITS - 1:
                        r.then_inc(first_rows, 1)
                    if u in between:
                        between[u]()

            def ada_unit(b, u, g, at, first, last):
                pe.wait_ge(ada_landed[u % AR], ((b - 2) * 2 + u // AR + 1) * 16)
                if u == 0 and first:
                    pe.wait_ge(row_copied, g)
                four_chunks(u, ada_u[:, u % AR], at, first, last).then_inc(ada_used, 1)

            def ada_turn(g, blocks=1):
                pe.wait_ge(row_copied, g + 1)
                if not (isinstance(g, int) and g == 0):
                    pe.wait_ge(ada_ready, g)
                w = blocks * SEQS
                for m in range(MT):
                    r = mm(ps_adat[:, w * m:w * (m + 1)], ada_row[:, m * P:(m + 1) * P],
                           cst[:, C_SEL:C_SEL + w], start=True, stop=True)
                r.then_inc(adat_ready, 1)

            pe.sem_inc(part_done, HL * MT)
            pe.sem_inc(ada_used, AR)
            pe.wait_ge(c_landed, 3 * 16)
            for t in range(NT):
                r = nc.tensor.transpose(ps_adat[:, SEQS * t:SEQS * (t + 1)], raw[0:SEQS, 3, t * P:(t + 1) * P],
                                        ident[0:SEQS, 0:SEQS])
            r.then_inc(c_t_psum, 1)
            pe.wait_ge(c_t_ready, 1)
            first_block(0, {1: hist_sums, 2: hist_turn})
            pe.wait_ge(vec_landed, len(VECTORS) * 16)
            nc.tensor.transpose(ps_a[:, 0:P], ada_row[:, 0:P], ident)
            nc.tensor.transpose(ps_a[:, P:2 * P], ada_row[:, P:2 * P], ident)
            nc.tensor.transpose(ps_a[:, 2 * P:V_ALL], ada_row[0:V_ALL - 2 * P, 2 * P:3 * P],
                                ident[0:NT, 0:NT]).then_inc(vec_psum, 1)
            def turn_x(tiles):
                for t in tiles:
                    if t >= len(x_bank):
                        pe.wait_ge(x_ready, t - len(x_bank) + 1)
                    b, cols = x_bank[t % len(x_bank)], slice(t * P, (t + 1) * P)
                    for k in range(2):
                        nc.tensor.transpose(b[:, k * P:(k + 1) * P], x_rows[:, k, cols], ident)
                    nc.tensor.transpose(b[:, PROMPT:TOK], x_sample[:, cols],
                                        ident[0:NS, 0:NS]).then_inc(x_psum, 1)

            pe.wait_ge(x_landed, 3 * 16)
            turn_x(range(KC))
            ada_turn(0)
            first_block(1)
            ada_turn(1)
            pe.wait_ge(rest_landed, 2 * 16)
            pe.wait_ge(vec_ready, 1)
            pe.wait_ge(hist_ready, 1)
            turn_x(range(KC, NT))

            def in_unit(q, i, j):
                unit(j, q * 16 + i * 4 + j, q * 64 + i * 16 + 4 * j, (U, q * 8), (U, q * 8 + KC))

            with pe.Fori(0, 3) as q:
                with pe.Fori(0, 2) as h:
                    for e in range(2):
                        for j in range(4):
                            ada_unit(q * 4 + h * 2 + e + 2, j, q * 2 + h + 2, SEQS * (e + 1), e == 0, e == 1)
                            pe.wait_ge(u_ready, q + 1)
                            in_unit(q, h * 2 + e, j)
                    ada_turn(q * 2 + h + 2, 2)
            pe.wait_ge(u_ready, 4)
            with pe.Fori(0, 2) as h:
                for e in range(2):
                    for j in range(4):
                        ada_unit(h * 2 + e + A_LAST, j, h + G_LAST, SEQS * (e + 1), e == 0, e == 1)
                        in_unit(3, h * 2 + e, j)
                ada_turn(h + G_LAST, 2)

            pe.wait_ge(pooled_ready, 1)
            for g in range(4):
                pe.wait_ge(unit_split, split_done(U_GRP + g))
                for m in range(2):
                    t = 2 * g + m
                    pe.wait_ge(psum_free, bank_free(T_GRP + t))
                    for c in range(2):
                        k = 2 * g + c
                        r = three(bank[t % BANKS][:, 0:TOK], w_of(g % HL, c, m, 2 * P), U[:, POOL_HI + k, :],
                                  U[:, POOL_LO + k, :], c == 0, c == 1)
                    r.then_inc(part_done, MT // 2)

            pe.wait_ge(proj_ready, 1)
            for t in range(PT):
                b, cols = (ps_a, ps_b)[t // 4], slice(t % 4 * P, t % 4 * P + P)
                nc.tensor.transpose(b[0:HIST + NS, cols], PB[:, Z + t, PROMPT - HIST:TOK], ident)
                r = mm(b[V_AT:V_AT + CH + NS, cols], PB[:, CC + t, PROMPT - CH:TOK], ident, start=True, stop=True)
            r.then_inc(state_psum, 1)

            def up_block(n, with_ada=True):
                for j in range(4):
                    if with_ada:
                        ada_unit(n + A_UP, j, G_UP, n * SEQS, n == 0, n == 2)
                    k = KC * (j % 2)
                    hi, lo = (((U, POOL_HI + k), (U, POOL_LO + k)), ((U, CONV_HI + k), (H, XC + k)))[j // 2]
                    if j < 2:
                        pe.wait_ge(yp_ready, j + 1)
                    else:
                        pe.wait_ge(yc_ready, 1)
                    unit(j, n * 4 + U_UP + j, n * 8 + T_UP + 4 * (j // 2), hi, lo, j % 2 == 0, j % 2 == 1)

            for n in range(3):
                up_block(n)
            ada_turn(G_UP, 3)
            up_block(3, with_ada=False)

            def pe_early_mean(l):
                pe.wait_ge(ln_in, 2 * l + 1)
                mm(ps_a[:, 0:TOK], ones, early_sum, start=True, stop=True).then_inc(ln_mean, 1)

            def pe_early_moment(l):
                pe.wait_ge(ln_sums, 2 * l + 1)
                mm(ps_b[:, 0:TOK], ones, G[:, NT, :], start=True, stop=False)

            def wo_block(n, with_ada=True, early={}):
                for j in range(4):
                    if with_ada:
                        ada_unit(n + A_WO, j, G_WO, n * SEQS, n == 0, n == 2)
                    pe.wait_ge(mixed_ready, j + 1)
                    unit(j, n * 4 + U_WO + j, n * 4 + T_WO, (H, MIX_HI + KC * j), (M, KC * j),
                         j == 0, j == 3, early.get(j))
            pe.wait_ge(avg_ready, 1)
            for n in range(3):
                wo_block(n)
            ada_turn(G_WO, 3)
            wo_block(3, with_ada=False, early={0: lambda: pe_early_mean(0), 3: lambda: pe_early_moment(0)})

            def norm(l):
                pe.wait_ge(ln_in, 2 * l + 2)
                mm(ps_ada[:, 0:TOK], ones, last_sum, start=True, stop=True).then_inc(ln_mean, 1)
                pe.wait_ge(ln_sums, 2 * l + 2)
                mm(ps_b[:, 0:TOK], ones, G[:, NT + 1, :], start=False, stop=True).then_inc(ln_moment, 1)

            norm(0)

            def ff1_block(q, i):
                for j in range(4):
                    pe.wait_ge(u2_ready, j + 1)
                    unit(j, q * 32 + i * 4 + U_FF + j, q * 32 + i * 4 + T_FF, (U, 8 * j), (U, 8 * j + KC), j == 0, j == 3)

            def ff2_block(q, i, early={}):
                for j in range(4):
                    pe.wait_ge(h_ready, q * 4 + j + 1)
                    unit(j, q * 32 + i * 4 + U_FF + 16 + j, q * 32 + i * 4 + T_FF + 16, (H, KC * j), (H, H_LO + KC * j),
                         j == 0, j == 3, early.get(j))

            with pe.Fori(0, 3) as q:
                with pe.Fori(0, 4) as i:
                    ff1_block(q, i)
                with pe.Fori(0, 4) as i:
                    ff2_block(q, i)
            with pe.Fori(0, 4) as i:
                ff1_block(3, i)
            with pe.Fori(0, 3) as i:
                ff2_block(3, i)
            ff2_block(3, 3, early={0: lambda: pe_early_mean(1), 3: lambda: pe_early_moment(1)})
            norm(1)
            for c in range(4):
                if c < 3:
                    pe.wait_ge(y_tiles, c + 1)
                else:
                    pe.wait_ge(y_tail, 1)
                for t in range(3):
                    k = 3 * c + t
                    if k >= len(y_bank):
                        wait_y_copied(pe, *divmod(k - len(y_bank), 3))
                    n, at = (P, t * P) if t < 2 else (NS, PROMPT)
                    for m in range(MT):
                        r = nc.tensor.transpose(y_bank[k % len(y_bank)][0:n, m * P:(m + 1) * P],
                                                X[:, MT * c + m, at:at + n], ident)
                    r.then_inc(y_psum, 1)


_INS = ["x_prompt", "x_sample", "state_pool", "state_conv", "c_prompt", "c_sample", "w_ada", "b_ada", "w_in",
        "pool_grp_w", "pool_scale", "conv_w", "w_pool_up", "w_conv_up", "w_o", "ln1_g", "ln1_b", "w_ff1", "b_ff1",
        "w_ff2", "b_ff2", "ln2_g", "ln2_b"]
_OUTS = {"y_prompt": (1, PROMPT, D), "y_sample": (NS, 1, D), "new_pool_prompt": (1, 1, HIST, D // 2),
         "new_conv_prompt": (1, 1, CH, D // 2), "new_pool_sample": (1, NS, HIST, D // 2),
         "new_conv_sample": (1, NS, CH, D // 2)}


def constants(np):
    c = np.zeros((P, C_ALL), np.float32)
    c[:, C_ID:C_ID + P] = np.eye(P, dtype=np.float32)
    for g in range(4):
        c[32 * g:32 * g + GROUP * SEQS, C_SEL:C_SEL + GROUP * SEQS] = np.eye(GROUP * SEQS, dtype=np.float32)
    for g, w in enumerate(POOL_W):
        for t in range(16):
            c[:, C_FIX + 16 * g + t] = w / min(w, t + 1)
        for s in range(NS):
            for h in range(HIST - (w - 1), HIST):
                c[s * HIST + h, C_HIST + NS * g + s] = 1.0
    return c


def kernel(**inputs):
    import numpy as _np
    import concourse.bacc as _bacc
    from concourse.bass_utils import run_bass_kernel_spmd as _run

    nc = _bacc.Bacc("TRN2", target_bir_lowering=False, num_devices=1)
    arrays = {f"in_{n}": _np.ascontiguousarray(inputs[n]) for n in _INS}
    arrays["in_cst"] = constants(_np)
    ins = {k[3:]: nc.dram_tensor(k, v.shape, F32, kind="ExternalInput").ap() for k, v in arrays.items()}
    outs = {n: nc.dram_tensor(f"out_{n}", s, F32, kind="ExternalOutput").ap() for n, s in _OUTS.items()}
    build_layer(nc, ins, outs)
    r = _run(nc, [arrays], core_ids=[0]).results[0]
    return tuple(r[f"out_{n}"] for n in _OUTS)
```
